# Optimizing a Trainium2 kernel written in Bass

```python
import math
import jax, jax.numpy as jnp
from jax import lax
import numpy as np

D_MODEL = 1024
BATCH = 1
SEQ = 128
DEPTH = 4
DEC_BATCH = 1
DEC_SEQ = 128
PAST_LEN = 128

GRID_W = 64
N_MIXERS = 3
N_DN = (DEPTH + 2) // 3
N_SC = (DEPTH + 1) // 3
N_NA = DEPTH // 3
N_DENSE = (DEPTH + 1) // 2
N_MOE = DEPTH // 2

DN_DK = 128
DN_DV = 128
DN_HEADS = D_MODEL // DN_DK
DN_CONV = 3
DN_CHUNK = 64

SC_CONV = 3

NA_HD = 64
NA_HEADS = D_MODEL // NA_HD
WIN_H = 8
WIN_W = 16
NA_QB = WIN_W
NA_KB = 2 * WIN_W

D_FF = 2816
N_EXPERTS = 8
TOP_K = 2
D_FF_EXPERT = 1408

EPS = 1e-6
NEG_INF = -1e30

kernel_name = "hybrid_diffusion_trunk_step"

def rms_norm(x, g):
    x32 = x.astype(jnp.float32)
    y = x32 * lax.rsqrt(jnp.mean(x32 * x32, axis=-1, keepdims=True) + EPS)
    return (y * g.astype(jnp.float32)).astype(x.dtype)

def l2_norm(x):
    x32 = x.astype(jnp.float32)
    return x32 * lax.rsqrt(jnp.sum(x32 * x32, axis=-1, keepdims=True) + EPS)

def modulate(x, g, shift, scale):
    return rms_norm(x, g) * (1 + scale) + shift

def conv_centred(x, w):
    k = w.shape[0]
    t = x.shape[1]
    p = k // 2
    xp = jnp.pad(x, ((0, 0), (p, p), (0, 0)))
    return sum(xp[:, j:j + t] * w[j] for j in range(k))

def chunk_gated_delta(q, k, v, g, beta, s0):
    b, h, t, dk = q.shape
    dv = v.shape[-1]
    c = DN_CHUNK
    n = t // c
    q = q.reshape(b, h, n, c, dk)
    k = k.reshape(b, h, n, c, dk)
    v = v.reshape(b, h, n, c, dv)
    g = jnp.cumsum(g.reshape(b, h, n, c), axis=-1)
    beta = beta.reshape(b, h, n, c)
    incl = jnp.tril(jnp.ones((c, c), dtype=bool))
    strict = jnp.tril(jnp.ones((c, c), dtype=bool), -1)
    diff = g[..., :, None] - g[..., None, :]
    decay = jnp.where(incl, jnp.exp(jnp.where(incl, diff, 0.0)), 0.0)
    kb = k * beta[..., None]
    a = jnp.where(strict, jnp.einsum('bhnid,bhnjd->bhnij', kb, k) * decay, 0.0)
    lower = a + jnp.eye(c, dtype=a.dtype)
    rhs = jnp.concatenate([v * beta[..., None], kb * jnp.exp(g)[..., None]], axis=-1)
    sol = lax.linalg.triangular_solve(lower, rhs, left_side=True, lower=True, unit_diagonal=True)
    u, w = sol[..., :dv], sol[..., dv:]
    qk = jnp.einsum('bhnid,bhnjd->bhnij', q, k) * decay

    def step(s, xs):
        q_c, k_c, u_c, w_c, g_c, qk_c = xs
        v_new = u_c - jnp.einsum('bhck,bhkv->bhcv', w_c, s)
        o_c = (jnp.einsum('bhck,bhkv->bhcv', q_c * jnp.exp(g_c)[..., None], s)
               + jnp.einsum('bhij,bhjv->bhiv', qk_c, v_new))
        g_last = g_c[..., -1:]
        s = (s * jnp.exp(g_last)[..., None]
             + jnp.einsum('bhck,bhcv->bhkv', k_c * jnp.exp(g_last - g_c)[..., None], v_new))
        return s, o_c

    xs = tuple(jnp.moveaxis(z, 2, 0) for z in (q, k, u, w, g, qk))
    s_final, o = lax.scan(step, s0, xs)
    o = jnp.moveaxis(o, 0, 2).reshape(b, h, t, dv)
    return o, s_final

def deltanet_mixer(h, s0, w_in, w_ab, conv_w, a_log, dt_bias, norm_g, w_out):
    b, t, _ = h.shape
    proj = h @ w_in
    qkv = jax.nn.silu(conv_centred(proj[..., :3 * D_MODEL], conv_w))
    z = proj[..., 3 * D_MODEL:]
    q, k, v = jnp.split(qkv, 3, axis=-1)

    def heads(x, d):
        return x.reshape(b, t, DN_HEADS, d).transpose(0, 2, 1, 3).astype(jnp.float32)

    q = l2_norm(heads(q, DN_DK)) * (DN_DK ** -0.5)
    k = l2_norm(heads(k, DN_DK))
    v = heads(v, DN_DV)
    ab = (h @ w_ab).astype(jnp.float32).reshape(b, t, 2, 2, DN_HEADS)
    g = -jnp.exp(a_log.astype(jnp.float32)) * jax.nn.softplus(ab[:, :, :, 0] + dt_bias.astype(jnp.float32))
    beta = jax.nn.sigmoid(ab[:, :, :, 1])
    g = g.transpose(0, 2, 3, 1)
    beta = beta.transpose(0, 2, 3, 1)
    s0 = s0.astype(jnp.float32)
    o_f, s_f = chunk_gated_delta(q, k, v, g[:, 0], beta[:, 0], s0[:, 0])

    def flip(x):
        return jnp.flip(x, axis=2)

    o_b, s_b = chunk_gated_delta(flip(q), flip(k), flip(v), flip(g[:, 1]), flip(beta[:, 1]), s0[:, 1])
    o = (o_f + flip(o_b)).transpose(0, 2, 1, 3)
    o = rms_norm(o, norm_g) * jax.nn.silu(z.reshape(b, t, DN_HEADS, DN_DV).astype(jnp.float32))
    out = o.reshape(b, t, D_MODEL).astype(h.dtype) @ w_out
    return out, jnp.stack([s_f, s_b], axis=1)

def shortconv_mixer(h, w_in, conv_w, w_out):
    bg, cg, u = jnp.split(h @ w_in, 3, axis=-1)
    return (bg * conv_centred(cg * u, conv_w)) @ w_out

def na_project(h, w_qkv, q_norm, k_norm):
    b, t, _ = h.shape
    q, k, v = jnp.split(h @ w_qkv, 3, axis=-1)

    def heads(x):
        return x.reshape(b, t, NA_HEADS, NA_HD).transpose(0, 2, 1, 3)

    return rms_norm(heads(q), q_norm), rms_norm(heads(k), k_norm), heads(v)

def merge_heads(o):
    b, h, t, d = o.shape
    return o.transpose(0, 2, 1, 3).reshape(b, t, h * d)

def na_context(h, w_qkv, q_norm, k_norm, w_out):
    q, k, v = na_project(h, w_qkv, q_norm, k_norm)
    s = jnp.einsum('bhqd,bhkd->bhqk', q, k).astype(jnp.float32) * (NA_HD ** -0.5)
    p = jax.nn.softmax(s, axis=-1).astype(v.dtype)
    o = jnp.einsum('bhqk,bhkd->bhqd', p, v)
    return merge_heads(o).astype(h.dtype) @ w_out, k, v

def na_latent(h, k_ctx, v_ctx, w_qkv, q_norm, k_norm, rpb, w_out):
    b, n, _ = h.shape
    rows = n // GRID_W
    kh = min(WIN_H, rows)
    ncb = GRID_W // NA_QB
    q, k, v = na_project(h, w_qkv, q_norm, k_norm)
    r = jnp.arange(rows)
    key_rows = jnp.clip(r - kh // 2, 0, rows - kh)[:, None] + jnp.arange(kh)
    c0 = jnp.arange(ncb) * NA_QB
    key_cols = jnp.clip(c0 - WIN_W // 2, 0, GRID_W - NA_KB)[:, None] + jnp.arange(NA_KB)
    q_cols = c0[:, None] + jnp.arange(NA_QB)
    col_start = jnp.clip(q_cols - WIN_W // 2, 0, GRID_W - WIN_W)[..., None]
    col_ok = (key_cols[:, None, :] >= col_start) & (key_cols[:, None, :] < col_start + WIN_W)
    mask = jnp.broadcast_to(col_ok[:, :, None, :], (ncb, NA_QB, kh, NA_KB)).reshape(ncb, NA_QB, kh * NA_KB)
    idx = (key_rows[:, None, :, None] * GRID_W + key_cols[None, :, None, :]).reshape(rows, ncb, kh * NA_KB)
    k_blk = jnp.take(k, idx, axis=2)
    v_blk = jnp.take(v, idx, axis=2)
    q_blk = q.reshape(b, NA_HEADS, rows, ncb, NA_QB, NA_HD)
    dr = key_rows - r[:, None] + (WIN_H - 1)
    dc = jnp.clip(key_cols[:, None, :] - q_cols[:, :, None] + (WIN_W - 1), 0, 2 * WIN_W - 2)
    bias = rpb[:, dr[:, None, None, :, None], dc[None, :, :, None, :]]
    bias = bias.reshape(NA_HEADS, rows, ncb, NA_QB, kh * NA_KB).astype(jnp.float32)
    scale = NA_HD ** -0.5
    s_loc = jnp.einsum('bhrcqd,bhrckd->bhrcqk', q_blk, k_blk).astype(jnp.float32) * scale + bias
    s_loc = jnp.where(mask, s_loc, NEG_INF)
    s_ctx = jnp.einsum('bhrcqd,bhld->bhrcql', q_blk, k_ctx).astype(jnp.float32) * scale
    p = jax.nn.softmax(jnp.concatenate([s_loc, s_ctx], axis=-1), axis=-1)
    nloc = kh * NA_KB
    o = (jnp.einsum('bhrcqk,bhrckd->bhrcqd', p[..., :nloc].astype(v.dtype), v_blk)
         + jnp.einsum('bhrcql,bhld->bhrcqd', p[..., nloc:].astype(v_ctx.dtype), v_ctx))
    o = o.reshape(b, NA_HEADS, n, NA_HD)
    return merge_heads(o).astype(h.dtype) @ w_out

def dense_ffn(h, w_gu, w_down):
    g, u = jnp.split(h @ w_gu, 2, axis=-1)
    return (jax.nn.silu(g) * u) @ w_down

def moe_ffn(h, router, w_gu, w_down):
    logits = (h @ router).astype(jnp.float32)
    top_v, top_i = lax.top_k(logits, TOP_K)
    w = jax.nn.softmax(top_v, axis=-1)
    combine = jnp.sum(jax.nn.one_hot(top_i, N_EXPERTS, dtype=jnp.float32) * w[..., None], axis=-2)
    gu = jnp.einsum('btd,edf->btef', h, w_gu)
    g, u = jnp.split(gu, 2, axis=-1)
    act = jax.nn.silu(g) * u * combine[..., None].astype(h.dtype)
    return jnp.einsum('btef,efd->btd', act, w_down)

def setup_inputs(seed: int = 0) -> dict:
    key = jax.random.key(seed)
    ks = iter(jax.random.split(key, 48))
    f32 = jnp.float32
    D = D_MODEL

    def nrm(shape, s):
        return jax.random.normal(next(ks), shape, f32) * s

    def gain(shape):
        return 1.0 + nrm(shape, 0.05)

    x_prompt = nrm((BATCH, SEQ, D), 1.0)
    x_sample = nrm((DEC_BATCH, DEC_SEQ, D), 1.0)
    state_dn = nrm((DEC_BATCH, N_DN, 2, DN_HEADS, DN_DK, DN_DV), 0.1)
    cache_na_k = nrm((DEC_BATCH, N_NA, NA_HEADS, PAST_LEN, NA_HD), 1.0)
    cache_na_v = nrm((DEC_BATCH, N_NA, NA_HEADS, PAST_LEN, NA_HD), 1.0)
    c = nrm((DEC_BATCH, D), 1.0)
    c_ctx = nrm((D,), 1.0)
    ada_w = nrm((DEPTH, D, 6 * D), D ** -0.5)
    ada_b = nrm((DEPTH, 6 * D), 0.02)
    norm_mix = gain((DEPTH, D))
    norm_ffn = gain((DEPTH, D))
    dn_w_in = nrm((N_DN, D, 4 * D), D ** -0.5)
    dn_w_ab = nrm((N_DN, D, 4 * DN_HEADS), D ** -0.5)
    dn_conv = nrm((N_DN, DN_CONV, 3 * D), DN_CONV ** -0.5)
    dn_a_log = jnp.log(jax.random.uniform(next(ks), (N_DN, 2, DN_HEADS), f32, 1.0, 16.0))
    dt = jnp.exp(jax.random.uniform(next(ks), (N_DN, 2, DN_HEADS), f32, math.log(1e-3), math.log(1e-1)))
    dn_dt_bias = dt + jnp.log(-jnp.expm1(-dt))
    dn_norm = gain((N_DN, DN_DV))
    dn_w_out = nrm((N_DN, D, D), D ** -0.5)
    sc_w_in = nrm((N_SC, D, 3 * D), D ** -0.5)
    sc_conv = nrm((N_SC, SC_CONV, D), SC_CONV ** -0.5)
    sc_w_out = nrm((N_SC, D, D), D ** -0.5)
    na_w_qkv = nrm((N_NA, D, 3 * D), D ** -0.5)
    na_q_norm = gain((N_NA, NA_HD))
    na_k_norm = gain((N_NA, NA_HD))
    na_rpb = nrm((N_NA, NA_HEADS, 2 * WIN_H - 1, 2 * WIN_W - 1), 0.1)
    na_w_out = nrm((N_NA, D, D), D ** -0.5)
    ff_w_gu = nrm((N_DENSE, D, 2 * D_FF), D ** -0.5)
    ff_w_down = nrm((N_DENSE, D_FF, D), D_FF ** -0.5)
    moe_router = nrm((N_MOE, D, N_EXPERTS), D ** -0.5)
    moe_w_gu = nrm((N_MOE, N_EXPERTS, D, 2 * D_FF_EXPERT), D ** -0.5)
    moe_w_down = nrm((N_MOE, N_EXPERTS, D_FF_EXPERT, D), D_FF_EXPERT ** -0.5)
    return {
        "x_prompt": x_prompt, "x_sample": x_sample,
        "state_dn": state_dn, "cache_na_k": cache_na_k, "cache_na_v": cache_na_v,
        "c": c, "c_ctx": c_ctx,
        "ada_w": ada_w, "ada_b": ada_b, "norm_mix": norm_mix, "norm_ffn": norm_ffn,
        "dn_w_in": dn_w_in, "dn_w_ab": dn_w_ab, "dn_conv": dn_conv, "dn_a_log": dn_a_log,
        "dn_dt_bias": dn_dt_bias, "dn_norm": dn_norm, "dn_w_out": dn_w_out,
        "sc_w_in": sc_w_in, "sc_conv": sc_conv, "sc_w_out": sc_w_out,
        "na_w_qkv": na_w_qkv, "na_q_norm": na_q_norm, "na_k_norm": na_k_norm,
        "na_rpb": na_rpb, "na_w_out": na_w_out,
        "ff_w_gu": ff_w_gu, "ff_w_down": ff_w_down,
        "moe_router": moe_router, "moe_w_gu": moe_w_gu, "moe_w_down": moe_w_down,
    }

def reference(x_prompt, x_sample, state_dn, cache_na_k, cache_na_v, c, c_ctx,
              ada_w, ada_b, norm_mix, norm_ffn,
              dn_w_in, dn_w_ab, dn_conv, dn_a_log, dn_dt_bias, dn_norm, dn_w_out,
              sc_w_in, sc_conv, sc_w_out,
              na_w_qkv, na_q_norm, na_k_norm, na_rpb, na_w_out,
              ff_w_gu, ff_w_down, moe_router, moe_w_gu, moe_w_down):
    xp = x_prompt
    xs = x_sample
    new_dn, new_k, new_v = [], [], []
    for i in range(DEPTH):
        m_ctx = jnp.split(jax.nn.silu(c_ctx) @ ada_w[i] + ada_b[i], 6, axis=-1)
        m_lat = [z[:, None, :] for z in jnp.split(jax.nn.silu(c) @ ada_w[i] + ada_b[i], 6, axis=-1)]
        hp = modulate(xp, norm_mix[i], m_ctx[0], m_ctx[1])
        hs = modulate(xs, norm_mix[i], m_lat[0], m_lat[1])
        kind = i % N_MIXERS
        j = i // N_MIXERS
        if kind == 0:
            wts = (dn_w_in[j], dn_w_ab[j], dn_conv[j], dn_a_log[j], dn_dt_bias[j], dn_norm[j], dn_w_out[j])
            s_zero = jnp.zeros((xp.shape[0], 2, DN_HEADS, DN_DK, DN_DV), jnp.float32)
            yp, st = deltanet_mixer(hp, s_zero, *wts)
            ys, _ = deltanet_mixer(hs, state_dn[:, j], *wts)
            new_dn.append(st)
        elif kind == 1:
            yp = shortconv_mixer(hp, sc_w_in[j], sc_conv[j], sc_w_out[j])
            ys = shortconv_mixer(hs, sc_w_in[j], sc_conv[j], sc_w_out[j])
        else:
            yp, kc, vc = na_context(hp, na_w_qkv[j], na_q_norm[j], na_k_norm[j], na_w_out[j])
            ys = na_latent(hs, cache_na_k[:, j], cache_na_v[:, j], na_w_qkv[j], na_q_norm[j],
                           na_k_norm[j], na_rpb[j], na_w_out[j])
            new_k.append(kc)
            new_v.append(vc)
        xp = xp + m_ctx[2] * yp
        xs = xs + m_lat[2] * ys
        hp = modulate(xp, norm_ffn[i], m_ctx[3], m_ctx[4])
        hs = modulate(xs, norm_ffn[i], m_lat[3], m_lat[4])
        f = i // 2
        if i % 2 == 0:
            fp = dense_ffn(hp, ff_w_gu[f], ff_w_down[f])
            fs = dense_ffn(hs, ff_w_gu[f], ff_w_down[f])
        else:
            fp = moe_ffn(hp, moe_router[f], moe_w_gu[f], moe_w_down[f])
            fs = moe_ffn(hs, moe_router[f], moe_w_gu[f], moe_w_down[f])
        xp = xp + m_ctx[5] * fp
        xs = xs + m_lat[5] * fs
    return (xp, xs, jnp.stack(new_dn, axis=1), jnp.stack(new_k, axis=1), jnp.stack(new_v, axis=1))


_drawn_inputs = setup_inputs


def setup_inputs(seed=0):
    import zlib

    import numpy as np

    out = dict(_drawn_inputs(seed))
    spreads = {}
    factors = {'na_q_norm': 7.883, 'na_rpb': 8.0}
    for name, (base, spread) in spreads.items():
        noise = np.random.default_rng([zlib.crc32(name.encode()), seed]).standard_normal(out[name].shape)
        drawn = base * np.exp(spread * noise) if base else spread * noise
        out[name] = __import__('jax').numpy.asarray(drawn.astype(out[name].dtype))
    for name, factor in factors.items():
        out[name] = (out[name] * factor).astype(out[name].dtype)
    return out
```

```python
from contextlib import ExitStack

import numpy as np

import concourse.bass as bass
from concourse import mybir

ALU = mybir.AluOpType
ACT = mybir.ActivationFunctionType
AX = mybir.AxisListType
F32 = mybir.dt.float32

P = 128
DM = 1024
KC = DM // P
T = 128
NT = 2 * T
DEPTH = 4
H = 8
NH = 16
HD = 64
DFF, DFE, NE, TOP_K = 2816, 1408, 8, 2
N_PAR = 12 + 8 + 3 + 4 + 2
GRID_W, WIN_H, WIN_W = 64, 8, 16
EPS = 1e-6
NEG = -1e30
SLOTS = 11
SLOT = 3072
SCR = 3
LEV = 6
KIND = ["dn", "sc", "na", "dn"]

C_ID, C_ONE, C_TF, C_TB, C_BLK, C_NAM, C_LEV = 0, 128, 256, 384, 512, 640, 768
C_RK = C_LEV + LEV * 2 * P
NCONST = C_RK + NE * NE


def shape_constants():
    c = np.zeros((P, NCONST), np.float32)
    i = np.arange(P)[:, None]
    j = np.arange(P)[None, :]
    c[:, C_ID:C_ID + P] = i == j
    c[:, C_ONE:C_ONE + P] = 1
    c[:, C_TF:C_TF + P] = i <= j
    c[:, C_TB:C_TB + P] = i >= j
    c[:, C_BLK:C_BLK + P] = (i // HD) == (j // HD)
    qc, kc = i % GRID_W, j % GRID_W
    start = np.clip(qc - WIN_W // 2, 0, GRID_W - WIN_W)
    c[:, C_NAM:C_NAM + P] = np.where((kc >= start) & (kc < start + WIN_W), 0.0, NEG)
    for l in range(LEV):
        b = 1 << l
        m = ((i // (2 * b)) == (j // (2 * b))) & ((i // b) % 2 == 1) & ((j // b) % 2 == 0)
        c[:, C_LEV + 2 * l * P:C_LEV + (2 * l + 1) * P] = m
        c[:, C_LEV + (2 * l + 1) * P:C_LEV + (2 * l + 2) * P] = m.T
    c[:, C_RK:] = (np.arange(NE)[:, None] > np.arange(NE)[None, :]).reshape(-1)
    return c


class Plan:

    def __init__(self):
        self.first, self.slot, self.before, self.arrived = [], [], [], []
        self.scratch, self.scratch_before, self.moe_slot, self.moe_before = {}, {}, {}, {}
        holder, landed, ptr, held, k = [None] * SLOTS, [0] * SLOTS, 0, [], 0

        def add(n, dmas):
            nonlocal ptr
            for _ in range(n):
                while ptr in held:
                    ptr = (ptr + 1) % SLOTS
                landed[ptr] += 16 * dmas
                self.slot.append(ptr)
                self.before.append(holder[ptr])
                self.arrived.append(landed[ptr])
                holder[ptr] = ("unit", len(self.slot) - 1)
                ptr = (ptr + 1) % SLOTS

        for l in range(DEPTH):
            f = {}
            if KIND[l] != "sc":
                s0 = ptr if ptr + SCR <= SLOTS else 0
                held = list(range(s0, s0 + SCR))
                self.scratch[l] = s0
                kinds = [holder[x] for x in held if holder[x]]
                self.scratch_before[l] = ("moe" if any(k == "moe" for k, _ in kinds) else
                                          max([m for _, m in kinds], default=None))
            for name, n, d in (("ada", 16, 1), ("in", {"dn": 16, "sc": 12, "na": 12}[KIND[l]], 1), ("out", 4, 1)):
                f[name] = len(self.slot)
                add(n, d)
            if KIND[l] != "sc":
                for s in held:
                    holder[s] = ("scratch", k)
                k += 1
            held = []
            f["ffn"] = len(self.slot)
            if l % 2 == 0:
                add(SLOTS * (DFF // DFE), 3)
            else:
                self.moe_slot[l] = [(ptr + j) % SLOTS for j in range(SLOTS)]
                self.moe_before[l] = [holder[x] for x in self.moe_slot[l]]
                for j, x in enumerate(self.moe_slot[l]):
                    holder[x] = ("moe", j)
            self.first.append(f)


PLAN = Plan()
DN_LAYERS = [l for l in range(DEPTH) if KIND[l] == "dn"]


def trunk(nc, a, outs):
    y_p, y_s, new_dn, new_k, new_v = outs
    with ExitStack() as ctx:
        def sb(name, shape):
            return ctx.enter_context(nc.sbuf_tensor(name, shape, F32))

        def sem(name):
            return ctx.enter_context(nc.semaphore(name))

        ring = sb("ring", [P, SLOTS, SLOT])
        xT = sb("xT", [P, KC, NT])
        hT = sb("hT", [P, KC, NT])
        cst = sb("cst", [P, NCONST])
        par = sb("par", [P, 9, P])
        mod = sb("mod", [P, 6 * KC, 2])
        gsc = sb("gsc", [P, 2, KC, 2])
        csil = sb("csil", [P, 2, KC])
        eps = sb("eps", [P, 1])
        rstd = sb("rstd", [P, NT])
        work = sb("work", [P, 10240])
        wab = sb("wab", [P, KC, 32])
        rout = sb("rout", [P, KC, NE])
        arow = sb("arow", [P, 32])
        sm = sb("sm", [P, 24, 32])
        ps = ctx.enter_context(nc.psum_tensor("ps", [P, 8, 512], F32))
        rpad = nc.dram_tensor("rpb_rows", (NH * 3, GRID_W * 127), F32, kind="Internal").ap()

        ident = cst[:, C_ID:C_ID + P]
        ones = cst[:, C_ONE:C_ONE + P]
        tri = [cst[:, C_TF:C_TF + P], cst[:, C_TB:C_TB + P]]
        blk64 = cst[:, C_BLK:C_BLK + P]

        def level(l, transposed=False):
            v = cst[:, C_LEV + 2 * l * P:C_LEV + (2 * l + 2) * P].rearrange("p (d n) -> p d n", d=2)
            if transposed:
                return [v[:, 1, :], v[:, 0, :]]
            return [v[:, 0, :], v[:, 1, :]]

        def wk(off, *dims):
            n = int(np.prod(dims))
            assert off + n <= 10240
            v = work[:, off:off + n]
            if len(dims) == 1:
                return v
            names = "abcd"[:len(dims)]
            return v.rearrange("p (%s) -> p %s" % (" ".join(names), " ".join(names)),
                               **dict(zip(names, dims)))

        def scratch(l, off, *dims):
            s0 = PLAN.scratch[l]
            v = ring[:, s0:s0 + SCR, :].rearrange("p s n -> p (s n)")[:, off:off + int(np.prod(dims))]
            assert off + int(np.prod(dims)) <= SCR * SLOT
            if len(dims) == 1:
                return v
            names = "abcd"[:len(dims)]
            return v.rearrange("p (%s) -> p %s" % (" ".join(names), " ".join(names)),
                               **dict(zip(names, dims)))

        mixT = wk(0, KC, NT)
        W1, W2, W3, W4 = 2048, 4096, 6144, 8192
        xtok = wk(0, 2, DM)
        prow = wk(2048, 9, P)
        gate_s = wk(W1, 3, NT)
        act_s = wk(W1 + 768, 3, NT)
        ada_rows = wk(W2, 2, 384)
        h_tok = wk(0, 2, DM)
        xg = wk(2048, KC, P)
        y_sum = wk(3072, KC, NT)
        y_e = wk(5120, DM)
        G_sel, G_cmb = wk(6144, 2, P), wk(6400, 2, P)
        S_cmb = wk(6656, NT)
        mg_s, ma_s, ma_T = wk(6912, 2, P), wk(7168, 2, P), wk(7424, 2, P)
        iota = wk(7680, P)
        slotv, combv = wk(7808, 2, 2 * NE + 1), wk(7842, 2, 2 * NE + 1)
        rk = wk(7876, 2, 2, NE * NE).rearrange("p a b (e f) -> p a b e f", e=NE)
        rounds = wk(8132, 1).bitcast(mybir.dt.int32)
        sc_b, sc_c = wk(W1, 2, 2, NT), wk(W1 + 1024, 2, 2, NT)
        sc_cu = wk(W2, 2, 2, 2, 130)
        sc_y = wk(W3, 2, 2, NT)
        qT, kT, zT = wk(W1, KC, NT), wk(W2, KC, NT), wk(W3, KC, NT)
        vtok = wk(W4, H, 2, P)
        ktok = hT[:, 0:4, :].rearrange("p a b -> p (a b)").rearrange("p (h n) -> p h n", h=H)
        na_bias = wk(W3, NH, P)
        na_vtok = wk(W4, 2, DM)
        rpb_sb = wk(W4, 127)

        slot_in = [sem(f"slot_in{i}") for i in range(SLOTS)]
        consts_in, x_in, par_in = sem("consts_in"), sem("x_in"), sem("par_in")
        small_in = sem("small_in")
        s0_in, ctx_in, rpb_in, rpb_rows, bias_in = (sem("s0_in"), sem("ctx_in"), sem("rpb_in"),
                                                    sem("rpb_rows"), sem("bias_in"))
        state_out = [sem("state_out0"), sem("state_out1")]
        kv_out, y_out = sem("kv_out"), sem("y_out")
        unit_done = sem("unit_done")
        p_pro, p_ss, p_gu, p_ab, p_at = (sem("p_" + n) for n in ("pro", "ss", "gu", "ab", "at"))
        d_ae, d_ar = sem("d_ae"), sem("d_ar")
        p_l2, p_vt, p_kt, p_ct, p_fin = (sem("p_" + n) for n in ("l2", "vt", "kt", "ct", "fin"))
        p_kk, p_m, p_mu, p_t, p_y, p_z, p_tz, p_o = (
            sem("p_" + n) for n in ("kk", "m", "mu", "t", "y", "z", "tz", "o"))
        p_s, p_pt, p_av = sem("p_s"), sem("p_pt"), sem("p_av")
        d_chain, d_pro, d_mod, d_x, d_h, d_prod, d_act, d_mix, d_conv, d_l2, d_vt, d_kt, d_ct = (
            sem("d_" + n) for n in ("chain", "pro", "mod", "x", "h", "prod", "act", "mix", "conv", "l2",
                                    "vt", "kt", "ct"))
        d_gate, d_fin = sem("d_gate"), sem("d_fin")
        d_dec, d_qd, d_m, d_u, d_r0, d_y, d_z, d_v = (
            sem("d_" + n) for n in ("dec", "qd", "m", "u", "r0", "y", "z", "v"))
        d_loc, d_max, d_p, d_pt = (sem("d_" + n) for n in ("loc", "max", "p", "pt"))
        a_chain, a_pro, a_sq, a_rs, a_h, a_pj, a_sl, a_silu, a_l2sq, a_l2n, a_l2r, a_gate = (
            sem("a_" + n) for n in ("chain", "pro", "sq", "rs", "h", "pj", "sl", "silu", "l2sq", "l2n", "l2r", "gate"))
        a_dec, a_qe, a_t, a_o = (sem("a_" + n) for n in ("dec", "qe", "t", "o"))
        a_cp, a_exp, a_pt, a_mix = (sem("a_" + n) for n in ("cp", "exp", "pt", "mix"))
        o_z = sem("o_z")
        moe_in = [sem(f"moe_in{x}") for x in range(SLOTS)]
        moe = {n: sem(f"m_{n}") for n in
             ("p_gu", "p_tr", "p_down", "p_sc", "p_st", "p_ga", "p_ht", "p_rt",
              "a_silu", "a_at", "a_y", "a_s", "a_xg", "a_ht", "a_lg",
              "d_act", "d_y", "d_sc", "d_gc", "d_g", "d_xg", "d_ht", "d_sel", "d_np", "d_lg")}

        ctx.enter_context(nc.allow_non_contiguous_dma("weight panels and small parameters"))

        IN_UNITS = {"dn": 16, "sc": 12, "na": 12}
        PJ0 = {0: 0, 1: 16, 2: 24, 3: 36}
        SL0 = {0: 0, 3: 12}
        L20 = {0: 0, 2: 12, 3: 20}
        VT0, KT0 = {0: 0, 2: 4, 3: 8}, {0: 0, 2: 2, 3: 4}
        MIX0 = {0: 0, 1: 4, 3: 8}
        SMALL = {0: 48, 1: 64, 3: 112}
        FFN0 = {0: 0, 2: 22}
        FB = [0, 1, 7]
        ROWS = [64, 64, 64, 64, 73, 24, 2, 73, 16]

        def last_in(j):
            return 3 if j >= 3 else {0: 2, 1: 2, 2: 5}[j]

        def nth(hd, k):
            return 2 * (LEV - 1) * (hd // 2) + 2 * k + hd % 2 + 1

        def ps4(b):
            return ps[:, b, :].rearrange("p (c n) -> p c n", c=4)

        def sv(i, *dims):
            n = int(np.prod(dims))
            v = sm[:, i, 0:n]
            if len(dims) == 1:
                return v
            names = "abcd"[:len(dims)]
            return v.rearrange("p (%s) -> p %s" % (" ".join(names), " ".join(names)),
                               **dict(zip(names, dims)))

        DTB, EXPA, U_, BCP, MAX0, AU, EX, LN1, EB, G_, B1, BETA, GC, TG, EG, KD, NEG_EG, BKD = range(18)
        LG, CMB, MX4, GQ, SEL, MX = range(18, 24)

        def AT(l, p): return scratch(l, 2560 * p, 4, P)
        def QD(l, p): return scratch(l, 2560 * p + 512, 4, P)
        def TT(l, p): return scratch(l, 2560 * p + 1024, 4, P)
        def UU(l, p): return scratch(l, 2560 * p + 1536, 4, P)
        def MM(l, p): return scratch(l, 2560 * p + 2048, 4, P)
        def S0(l): return scratch(l, 5120, 2, H, P)
        def STG(l, p): return scratch(l, 7168 + 256 * p, 2, P)
        def QE(l, p): return scratch(l, 7680 + 256 * p, 2, P)
        def R0(l, p): return scratch(l, 8192 + 256 * p, 2, P)
        def VS(l, p): return scratch(l, 8704 + 256 * p, 2, P)
        def CB(l, b): return scratch(l, 520 * b, 2, 2, 130)
        def CY(l, b): return scratch(l, 1040 + 512 * b, 2, NT)
        def SQ(l, b): return scratch(l, (7168 if KIND[l] == "na" else 2560) + 512 * b, 512)
        def RS(l, b): return scratch(l, (8192 if KIND[l] == "na" else 3584) + 512 * b, 512)
        def SS(p): return scratch(2, 4096 + 768 * p, 2, 384)
        def PT(p): return scratch(2, 5632 + 768 * p, 2, 384)
        kctok, vctx, kctxT = scratch(2, 0, NH * HD), scratch(2, 1024, NH, HD), scratch(2, 2048, KC, P)
        ktok_na = scratch(2, 3072, NH * HD)

        def pair(t, w):
            return t[:, 2 * w:2 * w + 2, :].rearrange("p c n -> p (c n)")

        block = ctx.enter_context(nc.Block())

        @block.sync
        def _(sp):
            sp.dma_start(cst[:], a["consts"]).then_inc(consts_in, 16)
            sp.dma_start(xtok[:, 0, :], a["x_prompt"][0]).then_inc(x_in, 16)
            sp.dma_start(xtok[:, 1, :], a["x_sample"][0]).then_inc(x_in, 16)

            done = [0]

            def slot_free(n):
                if PLAN.before[n] is None:
                    return
                free(*PLAN.before[n])

            def free(kind, m):
                if kind == "moe":
                    sp.wait_ge(moe["p_down"], done[0] * SLOTS + (m - SLOTS + 1))
                elif kind == "unit":
                    sp.wait_ge(unit_done, m + 1)
                elif m == 1:
                    sp.wait_ge(a_mix, KC)
                    sp.wait_ge(kv_out, 32)
                else:
                    sp.wait_ge(d_mix, 4 if m == 0 else 12)
                    for out in state_out:
                        sp.wait_ge(out, 64 if m == 0 else 128)

            def panel(n, w, n0, width):
                slot_free(n)
                dst = ring[:, PLAN.slot[n], 0:KC * width].rearrange("p (k n) -> p k n", k=KC)
                sp.dma_start(dst, w[:, n0:n0 + width].rearrange("(k p) n -> p k n", p=P)) \
                    .then_inc(slot_in[PLAN.slot[n]], 16)

            def ffn_unit(s, landed, gate, up, down):
                g = ring[:, s, 0:KC * P].rearrange("p (k n) -> p k n", k=KC)
                v = ring[:, s, KC * P:2 * KC * P].rearrange("p (k n) -> p k n", k=KC)
                sp.dma_start(g, gate).then_inc(landed, 16)
                sp.dma_start(v, up).then_inc(landed, 16)
                sp.dma_start(ring[:, s, 2 * KC * P:SLOT], down).then_inc(landed, 16)

            for l in range(DEPTH):
                f = PLAN.first[l]
                for i in range(16):
                    panel(f["ada"] + i, a["ada_w"][l], 384 * i, 384)
                w_in, w_out = {"dn": (a["dn_w_in"][l // 3], a["dn_w_out"][l // 3]),
                               "sc": (a["sc_w_in"][0], a["sc_w_out"][0]),
                               "na": (a["na_w_qkv"][0], a["na_w_out"][0])}[KIND[l]]
                for i in range(IN_UNITS[KIND[l]]):
                    c = 4 * (i % 3) + i // 3 if KIND[l] == "sc" else i
                    panel(f["in"] + i, w_in, 256 * c, 256)
                for i in range(4):
                    panel(f["out"] + i, w_out, 256 * i, 256)
                n0 = f["ffn"]

                def dense(it, j):
                    gu, dn = a["ff_w_gu"][l // 2], a["ff_w_down"][l // 2]
                    c = it * DFE + j * P
                    ffn_unit(PLAN.slot[n0 + j], slot_in[PLAN.slot[n0 + j]],
                             gu[:, bass.ds(c, P)].rearrange("(k p) n -> p k n", p=P),
                             gu[:, bass.ds(c + DFF, P)].rearrange("(k p) n -> p k n", p=P),
                             dn[bass.ds(c, P), :])

                def expert(it, j):
                    gu, dn = a["moe_w_gu"][l // 2], a["moe_w_down"][l // 2]
                    e, x = bass.ds(it, 1), PLAN.moe_slot[l][j]
                    ffn_unit(x, moe_in[x],
                             gu[e, :, j * P:(j + 1) * P].rearrange("e (k p) n -> p (e k) n", p=P),
                             gu[e, :, DFE + j * P:DFE + (j + 1) * P].rearrange("e (k p) n -> p (e k) n", p=P),
                             dn[e, j * P:(j + 1) * P, :].rearrange("e p n -> (e p) n"))

                if l % 2 == 0:
                    for j in range(SLOTS):
                        slot_free(n0 + j)
                        dense(0, j)
                    with sp.Fori(1, DFF // DFE) as it:
                        for j in range(SLOTS):
                            sp.wait_ge(unit_done, it * SLOTS + (n0 + j - SLOTS + 1))
                            dense(it, j)
                else:
                    for j in range(SLOTS):
                        if PLAN.moe_before[l][j]:
                            free(*PLAN.moe_before[l][j])
                        expert(0, j)
                    sp.wait_ge(moe["d_np"], l // 2 + 1)
                    n_more = sp.value_load(rounds[0:1, 0:1], min_val=NE - 1, max_val=2 * NE - 1)
                    with sp.Fori(0, n_more) as r:
                        for j in range(SLOTS):
                            sp.wait_ge(moe["p_down"], (done[0] + r) * SLOTS + (j + 1))
                            expert((r + 1) % NE, j)
                    done[0] = sp.snap(done[0] + n_more + 1)
            sp.wait_ge(d_fin, 2)
            sp.dma_start(y_p[0], xtok[:, 0, :]).then_inc(y_out, 16)
            sp.wait_ge(d_fin, 4)
            sp.dma_start(y_s[0], xtok[:, 1, :]).then_inc(y_out, 16)
            sp.wait_ge(y_out, 32)

        @block.gpsimd
        def _(po):
            def rows(k, r0, src):
                po.dma_start(prow[r0:r0 + src.shape[0], k, 0:src.shape[1]], src).then_inc(par_in, 16)

            for l in range(DEPTH):
                rows(l, 0, a["ada_b"][l].rearrange("(n p) -> n p", p=P))
                rows(l, 48, a["norm_mix"][l].rearrange("(n p) -> n p", p=P))
                rows(l, 56, a["norm_ffn"][l].rearrange("(n p) -> n p", p=P))
            for l in DN_LAYERS:
                for j in range(3):
                    rows(4 + l, 24 * j, a["dn_conv"][l // 3, j].rearrange("(n p) -> n p", p=P))
                rows(4 + l, 72, a["dn_norm"][l // 3:l // 3 + 1])
            for j in range(3):
                rows(5, 8 * j, a["sc_conv"][0, j].rearrange("(n p) -> n p", p=P))
            for half in range(2):
                for r, nm in enumerate(("na_q_norm", "na_k_norm")):
                    po.dma_start(prow[r:r + 1, 6, half * HD:(half + 1) * HD], a[nm]).then_inc(par_in, 16)
            rows(8, 0, a["c_ctx"].rearrange("(n p) -> n p", p=P))
            rows(8, 8, a["c"][0].rearrange("(n p) -> n p", p=P))

            def dn_small(j):
                po.dma_start(wab[:], a["dn_w_ab"][j].rearrange("(k p) n -> p k n", p=P)).then_inc(small_in, 16)
                po.dma_start(arow[0:1, 0:16], a["dn_a_log"][j:j + 1].rearrange("o d h -> o (d h)")) \
                    .then_inc(small_in, 16)
                po.dma_start(arow[0:1, 16:32], a["dn_dt_bias"][j:j + 1].rearrange("o d h -> o (d h)")) \
                    .then_inc(small_in, 16)

            def dn_states(l):
                i, j = DN_LAYERS.index(l), l // 3
                if isinstance(PLAN.scratch_before[l], int):
                    po.wait_ge(unit_done, PLAN.scratch_before[l] + 1)
                for d in range(2):
                    po.dma_start(S0(l)[:, d], a["state_dn"][0, j, d].rearrange("h k v -> k h v")) \
                        .then_inc(s0_in, 16)
                for h in range(H):
                    po.wait_ge(a_o, H * i + h + 1)
                    po.dma_start(new_dn[0, j, :, h].rearrange("d k v -> k d v"), STG(l, h % 2)) \
                        .then_inc(state_out[h % 2], 16)

            dn_small(0)
            po.memset(rpb_sb[0:48, :], 0.0).then_inc(o_z, 1)
            po.wait_ge(o_z, 1)
            for h in range(NH):
                po.dma_start(rpb_sb[3 * h:3 * h + 3, 48:79], a["na_rpb"][0, h, WIN_H - 2:WIN_H + 1, :]) \
                    .then_inc(rpb_in, 16)
            po.wait_ge(rpb_in, 16 * NH)
            po.dma_start(rpad.rearrange("r (c u) -> r c u", u=127),
                         rpb_sb[0:48, None, :].to_broadcast([48, GRID_W, 127])).then_inc(rpb_rows, 16)
            dn_states(0)
            po.dma_start(rout[:], a["moe_router"][0].rearrange("(k p) n -> p k n", p=P)).then_inc(small_in, 16)
            assert PLAN.scratch_before[2] == "moe"
            po.wait_ge(d_x, 16)
            po.wait_ge(rpb_rows, 16)
            for r in range(2):
                for r2 in range(2):
                    src = bass.AP(rpad.tensor, (r2 - r + 1) * GRID_W * 127 + 63,
                                  [[126, GRID_W], [3 * GRID_W * 127, NH], [1, GRID_W]])
                    po.dma_start(na_bias[r * GRID_W:(r + 1) * GRID_W, :, r2 * GRID_W:(r2 + 1) * GRID_W],
                                 src).then_inc(bias_in, 16)
            po.dma_start(kctok.rearrange("p (h d) -> p h d", h=NH),
                         a["cache_na_k"][0, 0].rearrange("h l d -> l h d")).then_inc(ctx_in, 16)
            po.dma_start(vctx, a["cache_na_v"][0, 0].rearrange("h l d -> l h d")).then_inc(ctx_in, 16)
            po.wait_ge(d_vt, VT0[2] + 2)
            po.dma_start(new_v[0, 0].rearrange("h t d -> t h d"),
                         na_vtok[:, 0, :].rearrange("p (h d) -> p h d", h=NH)).then_inc(kv_out, 16)
            po.wait_ge(d_kt, KT0[2] + 2)
            po.dma_start(new_k[0, 0].rearrange("h t d -> t h d"),
                         ktok_na.rearrange("p (h d) -> p h d", h=NH)).then_inc(kv_out, 16)
            po.wait_ge(kv_out, 32)
            dn_small(1)
            dn_states(3)
            po.dma_start(rout[:], a["moe_router"][1].rearrange("(k p) n -> p k n", p=P)).then_inc(small_in, 16)
            for out in state_out:
                po.wait_ge(out, 8 * H * len(DN_LAYERS))

        @block.tensor
        def _(pe):
            def mm(out, lhsT, rhs, start=True, stop=True, **kw):
                return pe.matmul(out, lhsT, rhs, start=start, stop=stop, **kw)

            def arrive(n):
                pe.wait_ge(slot_in[PLAN.slot[n]], PLAN.arrived[n])

            pe.wait_ge(consts_in, 16)
            pe.wait_ge(x_in, 32)
            for b in range(4):
                for k in range(2):
                    for g in range(2):
                        c = 2 * b + k
                        ins = pe.transpose(ps[:, 2 + b, (2 * k + g) * P:(2 * k + g + 1) * P],
                                           xtok[:, g, c * P:(c + 1) * P], ident)
                ins.then_inc(p_pro, 1)
            pe.wait_ge(par_in, 16 * N_PAR)
            for k, r in enumerate(ROWS):
                ins = pe.transpose(ps[:, [0, 1, 6][k // 4], (k % 4) * P:(k % 4) * P + r],
                                   prow[0:r, k, :], ident[0:r, 0:r])
            ins.then_inc(p_pro, 1)
            pe.wait_ge(a_pro, 1)

            def ada(l):
                f = PLAN.first[l]["ada"]
                pe.wait_ge(d_mod, l)
                for i in range(17):
                    if i < 16:
                        arrive(f + i)
                        if i >= 2:
                            pe.wait_ge(d_ae, 16 * l + i - 1)
                        w = ring[:, PLAN.slot[f + i], :].rearrange("p (k n) -> p k n", k=KC)
                        for m in range(2):
                            for j in range(4):
                                k = 2 * j + m
                                ins = mm(ps[32 * j:32 * j + 2, i % 2, 0:384], csil[:, :, k], w[:, k, :],
                                         m == 0, m == 1)
                        ins.then_inc(unit_done, 1)
                    if i >= 1:
                        t = i - 1
                        pe.wait_ge(d_ae, 16 * l + t + 1)
                        if t >= 2:
                            pe.wait_ge(d_ar, 16 * l + t - 1)
                        for c in range(3):
                            ins = pe.transpose(ps[:, 6 + t % 2, c * P:(c + 1) * P],
                                               ada_rows[:, t % 2, c * P:(c + 1) * P], ident)
                        ins.then_inc(p_at, 1)

            def norm(s):
                pe.wait_ge(d_ar, 16 * (s // 2 + 1))
                for k in range(KC):
                    if k % 4 == 0:
                        pe.wait_ge(a_sq, 2 * s + k // 4 + 1)
                    ins = mm(ps[:, 7, 0:NT], ones, hT[:, k, :], k == 0, k == KC - 1)
                ins.then_inc(p_ss, 1)

            def project(n, b, rhs, s=None):
                arrive(n)
                w = ring[:, PLAN.slot[n], 0:KC * 256].rearrange("p (k n) -> p k n", k=KC)
                for c in range(2):
                    for k in range(KC):
                        if s is not None and c == 0:
                            pe.wait_ge(d_h, 8 * s + k + 1)
                            pe.wait_ge(a_h, 8 * s + k + 1)
                        ins = mm(ps[:, b, c * NT:(c + 1) * NT], w[:, k, c * P:(c + 1) * P], rhs[:, k, :],
                                 k == 0, k == KC - 1)
                ins.then_inc(unit_done, 1)

            def out_proj(l):
                for i in range(4):
                    if i >= 2:
                        pe.wait_ge(d_x, 8 * l + i - 1)
                    project(PLAN.first[l]["out"] + i, i % 2, mixT)

            def sums(l, w, src_bank, mat):
                pe.wait_ge(a_l2sq, L20[l] + w + 1)
                if w >= 2:
                    pe.wait_ge(a_l2n, L20[l] + w - 1)
                mm(ps[:, src_bank, :], mat, SQ(l, w % 2)).then_inc(p_l2, 1)

            def deltanet(l):
                i = DN_LAYERS.index(l)
                u = PLAN.first[l]["in"]
                for w in range(16):
                    if w >= 2:
                        pe.wait_ge(a_pj, PJ0[l] + w - 1)
                    project(u + w, w % 2, hT, 2 * l if w == 0 else None)
                pe.wait_ge(small_in, SMALL[l])
                for g in range(2):
                    for k in range(KC):
                        mm(ps[:, 6, 32 * g:32 * g + 32], hT[:, k, g * P:(g + 1) * P], wab[:, k, :],
                           k == 0, k == KC - 1)
                mm(ps[:, 6, 64:96], ones[0:1, :], arow[0:1, :]).then_inc(p_ab, 1)
                pe.wait_ge(a_sl, SL0[l] + 12)
                for m in range(4):
                    if m >= 2:
                        pe.wait_ge(d_vt, VT0[l] + m - 1)
                    for c in range(4):
                        h, g = 2 * m + c // 2, c % 2
                        ins = pe.transpose(ps[:, 4 + m % 2, c * P:(c + 1) * P],
                                           mixT[:, h, g * P:(g + 1) * P], ident)
                    ins.then_inc(p_vt, 1)
                for w in range(8):
                    sums(l, w, 2 + w % 2, ones)
                pe.wait_ge(d_vt, VT0[l] + 4)
                pe.wait_ge(d_l2, L20[l] + 8)
                for m in range(2):
                    for c in range(4):
                        ins = pe.transpose(ps[:, 4 + m, c * P:(c + 1) * P], kT[:, 4 * m + c, 0:P], ident)
                    ins.then_inc(p_kt, 1)
                pe.wait_ge(d_gate, 3 * i + 2)
                for d in range(2):
                    mm(ps[:, 7, 16 * d:16 * d + 16], tri[d], sv(G_, 32)[:, 16 * d:16 * d + 16])
                mm(ps[:, 7, 32:64], ones, sv(G_, 32)).then_inc(p_ab, 1)
                pe.wait_ge(s0_in, 32 * (i + 1))
                pe.wait_ge(d_kt, KT0[l] + 2)

                def combos():
                    for d in range(2):
                        for g in range(2):
                            yield 2 * d + g, d, g

                def cols(b, c):
                    return ps[:, b, c * P:(c + 1) * P]

                def s_kk(h, p, hd, X, Y, Z):
                    if hd % H < 2:
                        pe.wait_ge(d_gate, 3 * i + 3)
                    if h >= 2:
                        pe.wait_ge(a_o, hd - 1)
                    for c, d, g in combos():
                        k = (2 * d + g) * H + h
                        mm(cols(X, c), sv(G_, 32)[:, k:k + 1].to_broadcast([P, P]), tri[d])
                    for g in range(2):
                        q, kk = qT[:, h, g * P:(g + 1) * P], kT[:, h, g * P:(g + 1) * P]
                        mm(cols(Y, g), kk, kk)
                        mm(cols(Y, 2 + g), kk, q)
                    for d in range(2):
                        ins = mm(cols(Z, d), kT[:, h, P:NT], S0(l)[:, d, h, :])
                    ins.then_inc(p_kk, 1)

                def s_t(lev):
                    def f(h, p, hd, X, Y, Z):
                        if lev == 0:
                            pe.wait_ge(d_qd, hd + 1)
                            pe.wait_ge(a_qe, hd + 1)
                        else:
                            pe.wait_ge(d_u, nth(hd, lev - 1))
                        for c, d, g in combos():
                            ins = pe.transpose(cols(X, c), UU(l, p)[:, c, :], ident)
                        ins.then_inc(p_t, 1)
                    return f

                def s_m(lev):
                    def f(h, p, hd, X, Y, Z):
                        pe.wait_ge(a_t, nth(hd, lev - 1))
                        for c, d, g in combos():
                            ins = mm(cols(X, c), AT(l, p)[:, c, :], TT(l, p)[:, c, :])
                        ins.then_inc(p_m, 1)
                    return f

                def s_mu(lev):
                    def f(h, p, hd, X, Y, Z):
                        pe.wait_ge(d_m, nth(hd, lev - 1))
                        for c, d, g in combos():
                            ins = mm(cols(Y, c), MM(l, p)[:, c, :], UU(l, p)[:, c, :])
                        ins.then_inc(p_mu, 1)
                    return f

                def s_y(h, p, hd, X, Y, Z):
                    pe.wait_ge(d_u, nth(hd, LEV - 2))
                    pe.wait_ge(d_r0, hd + 1)
                    for c, d, g in combos():
                        ins = mm(cols(X, c), UU(l, p)[:, c, :], vtok[:, h, 0, :] if g == 0 else R0(l, p)[:, d, :])
                    ins.then_inc(p_y, 1)

                def s_z(h, p, hd, X, Y, Z):
                    pe.wait_ge(d_y, hd + 1)
                    for c, d, g in combos():
                        src, dst = (slice(0, 64), slice(64, 128)) if d == 0 else (slice(64, 128), slice(0, 64))
                        ins = mm(ps[dst, Y, c * P:(c + 1) * P], AT(l, p)[src, c, dst], MM(l, p)[src, c, :])
                    ins.then_inc(p_z, 1)

                def s_tz(h, p, hd, X, Y, Z):
                    pe.wait_ge(d_z, hd + 1)
                    for c, d, g in combos():
                        dst = slice(64, 128) if d == 0 else slice(0, 64)
                        ins = mm(ps[dst, X, c * P:(c + 1) * P], UU(l, p)[dst, c, dst], TT(l, p)[dst, c, :])
                    ins.then_inc(p_tz, 1)

                def s_o(h, p, hd, X, Y, Z):
                    pe.wait_ge(d_v, hd + 1)
                    for g in range(2):
                        terms = [(MM(l, p)[:, 2 * d + g, :], QD(l, p)[:, 2 * d + g, :]) for d in range(2)]
                        if g == 1:
                            terms += [(S0(l)[:, d, h, :], QE(l, p)[:, d, :]) for d in range(2)]
                        for t, (x, y) in enumerate(terms):
                            mm(cols(Y, g), x, y, t == 0, t == len(terms) - 1)
                    for d in range(2):
                        ins = mm(cols(Y, 2 + d), ktok[:, h, :], VS(l, p)[:, d, :])
                    ins.then_inc(p_o, 1)

                steps = [s_kk, s_t(0)]
                for lev in range(1, LEV):
                    steps += [s_m(lev), s_mu(lev)] + ([s_t(lev)] if lev < LEV - 1 else [])
                steps += [s_y, s_z, s_tz, s_o]
                for h0 in range(0, H, 2):
                    for step in steps:
                        for p in range(2):
                            step(h0 + p, p, H * i + h0 + p, 2 + 2 * p, 3 + 2 * p, 6 + p)
                for m in range(4):
                    sums(l, 8 + m, 2 + m % 2, ones)
                pe.wait_ge(d_mix, MIX0[l] + 4)

            def shortconv(l):
                u = PLAN.first[l]["in"]
                for n in range(12):
                    j, part = n // 3, n % 3
                    if n >= 2:
                        m = n - 2
                        if m % 3 == 2:
                            pe.wait_ge(d_prod, m // 3 + 1)
                        else:
                            pe.wait_ge(a_pj, PJ0[l] + 2 * (m // 3) + m % 3 + 1)
                    project(u + n, n % 2, hT, 2 * l if n == 0 else None)
                pe.wait_ge(d_mix, MIX0[l] + 4)

            def attention(l):
                u = PLAN.first[l]["in"]
                for w in range(12):
                    if w >= 2:
                        pe.wait_ge(a_pj, PJ0[l] + w - 1)
                    project(u + w, w % 2, hT, 2 * l if w == 0 else None)
                pe.wait_ge(ctx_in, 32)
                for m in range(2):
                    for c in range(4):
                        ins = pe.transpose(ps[:, 6 + m, c * P:(c + 1) * P],
                                           kctok[:, (4 * m + c) * P:(4 * m + c + 1) * P], ident)
                    ins.then_inc(p_ct, 1)
                pe.wait_ge(a_pj, PJ0[l] + 12)
                for m in range(4):
                    if m >= 2:
                        pe.wait_ge(d_vt, VT0[l] + m - 1)
                    for c in range(4):
                        ch, g = 4 * (m % 2) + c, m // 2
                        ins = pe.transpose(ps[:, 4 + m % 2, c * P:(c + 1) * P],
                                           mixT[:, ch, g * P:(g + 1) * P], ident)
                    ins.then_inc(p_vt, 1)
                for w in range(8):
                    sums(l, w, 2 + w % 2, blk64)
                pe.wait_ge(d_vt, VT0[l] + 4)
                pe.wait_ge(d_l2, L20[l] + 8)
                for m in range(2):
                    for c in range(4):
                        ins = pe.transpose(ps[:, 4 + m, c * P:(c + 1) * P], kT[:, 4 * m + c, 0:P], ident)
                    ins.then_inc(p_kt, 1)
                pe.wait_ge(d_ct, 2)
                pe.wait_ge(d_kt, KT0[l] + 2)

                def scores(j):
                    p = j % 2
                    if j >= 2:
                        pe.wait_ge(d_loc, j - 1)
                        pe.wait_ge(a_cp, j - 1)
                    for hh in range(2):
                        r, b = slice(64 * hh, 64 * hh + 64), 2 * p + hh
                        mm(ps[:, b, 0:128], qT[r, j, P:NT], kT[r, j, P:NT])
                        mm(ps[:, b, 128:256], qT[r, j, P:NT], kctxT[r, j, :])
                        ins = mm(ps[:, b, 256:384], qT[r, j, 0:P], kT[r, j, 0:P])
                    ins.then_inc(p_s, 1)

                def values(j):
                    p = j % 2
                    pe.wait_ge(d_p, j + 1)
                    if j >= 1:
                        pe.wait_ge(a_pt, j)
                        pe.wait_ge(d_pt, j)
                    for hh in range(2):
                        for t in range(3):
                            ins = pe.transpose(ps[:, 4 + hh, t * P:(t + 1) * P],
                                               SS(p)[:, hh, t * P:(t + 1) * P], ident)
                    ins.then_inc(p_pt, 1)
                    pe.wait_ge(a_pt, j + 1)
                    pe.wait_ge(d_pt, j + 1)
                    if j >= 2:
                        pe.wait_ge(a_mix, j - 1)
                    for hh in range(2):
                        r, h = slice(64 * hh, 64 * hh + 64), 2 * j + hh
                        c = slice(h * HD, (h + 1) * HD)
                        mm(ps[r, 6 + p, P:NT], na_vtok[:, 1, c], PT(p)[:, hh, 0:P], True, False)
                        mm(ps[r, 6 + p, P:NT], vctx[:, h, :], PT(p)[:, hh, P:2 * P], False, True)
                        ins = mm(ps[r, 6 + p, 0:P], na_vtok[:, 0, c], PT(p)[:, hh, 2 * P:3 * P])
                    ins.then_inc(p_av, 1)

                scores(0)
                for j in range(KC):
                    if j + 1 < KC:
                        scores(j + 1)
                    values(j)
                pe.wait_ge(a_mix, KC)

            done = [0]

            def experts(l):
                s, i, q0 = 2 * l + 1, l // 2, done[0]
                pe.wait_ge(d_h, 8 * s + 8)
                pe.wait_ge(a_h, 8 * s + 8)
                pe.wait_ge(small_in, SMALL[l] + (16 if l == 3 else 0))
                for g in range(2):
                    for k in range(KC):
                        ins = mm(ps[:, 2, 8 * g:8 * g + 8], hT[:, k, g * P:(g + 1) * P], rout[:, k, :],
                                 k == 0, k == KC - 1)
                ins.then_inc(moe["p_rt"], 1)
                for m in range(4):
                    for c in range(4):
                        g, k = m // 2, 4 * (m % 2) + c
                        ins = pe.transpose(ps[:, 4 + m, c * P:(c + 1) * P], hT[:, k, g * P:(g + 1) * P], ident)
                    ins.then_inc(moe["p_ht"], 1)
                pe.wait_ge(moe["d_sel"], i + 1)
                sel = sv(SEL, 2, NE)
                mm(ps[:, 3, 0:8], tri[0], sel[:, 0, :])
                mm(ps[:, 3, 8:16], tri[0], sel[:, 1, :], True, False)
                mm(ps[:, 3, 8:16], ones, sel[:, 0, :], False, True)
                mm(ps[:, 3, 16:24], ones, sel[:, 0, :], True, False)
                mm(ps[:, 3, 16:24], ones, sel[:, 1, :], False, True)
                mm(ps[:, 3, P:2 * P], ones, tri[0]).then_inc(moe["p_rt"], 1)
                pe.wait_ge(moe["d_np"], i + 1)
                n_more = pe.value_load(rounds[0:1, 0:1], min_val=NE - 1, max_val=2 * NE - 1)

                def gather(half):
                    for c in range(4):
                        k = 4 * half + c
                        for g in range(2):
                            ins = mm(ps[:, 4 + half, c * P:(c + 1) * P], h_tok[:, g, k * P:(k + 1) * P],
                                     G_sel[:, g, :], g == 0, g == 1)
                    ins.then_inc(moe["p_ga"], 1)

                pe.wait_ge(moe["a_ht"], 2 * i + 2)
                pe.wait_ge(moe["d_ht"], 2 * i + 2)
                pe.wait_ge(moe["d_g"], q0 + (i + 1))
                gather(0)
                gather(1)

                def gate_up(q, j, first):
                    x = PLAN.moe_slot[l][j]
                    pe.wait_ge(moe_in[x], q * 48 + 48)
                    if j == 0:
                        pe.wait_ge(moe["a_xg"], q + (i + 1))
                        pe.wait_ge(moe["d_xg"], q + (i + 1))
                    if not first or j >= 2:
                        pe.wait_ge(moe["d_act"], q * SLOTS + (j - 1 if j >= 2 else -j))
                    w = ring[:, x, 0:2 * KC * P].rearrange("p (v k n) -> p v k n", v=2, k=KC)
                    for k in range(KC):
                        ins = mm(ps[:, j % 2, 0:2 * P], xg[:, k, :], w[:, :, k, :], k == 0, k == KC - 1)
                    ins.then_inc(moe["p_gu"], 1)

                def turn(q, j, first):
                    pe.wait_ge(moe["d_act"], q * SLOTS + (j + 1))
                    if not first or j >= 2:
                        pe.wait_ge(moe["a_at"], q * SLOTS + (j - 1 if j >= 2 else -j))
                    pe.transpose(ps[:, 6 + j % 2, 0:P], ma_s[:, j % 2, :], ident).then_inc(moe["p_tr"], 1)

                def down(q, j, first):
                    pe.wait_ge(moe["a_at"], q * SLOTS + (j + 1))
                    if j == 0 and not first:
                        pe.wait_ge(moe["a_y"], q)
                        pe.wait_ge(moe["d_y"], q)
                    w = ring[:, PLAN.moe_slot[l][j], 2 * KC * P:SLOT]
                    for x in range(2):
                        ins = mm(ps[:, 2 + x, :], ma_T[:, j % 2, :], w[:, 512 * x:512 * x + 512],
                                 j == 0, j == SLOTS - 1)
                    ins.then_inc(moe["p_down"], 1)

                def scatter(q, m):
                    if m == 0:
                        pe.wait_ge(moe["a_y"], q + 1)
                        pe.wait_ge(moe["d_y"], q + 1)
                        pe.wait_ge(moe["a_s"], q + 1)
                    if m >= 2:
                        pe.wait_ge(moe["d_sc"], q * 4 + (m - 1))
                    for c in range(2):
                        k = 2 * m + c
                        ins = mm(ps[:, 4 + m % 2, c * NT:(c + 1) * NT], y_e[:, k * P:(k + 1) * P], S_cmb)
                    ins.then_inc(moe["p_sc"], 1)

                def body(q, first):
                    for j in range(SLOTS):
                        gate_up(q, j, first)
                        if j >= 1:
                            turn(q, j - 1, first)
                        elif not first:
                            turn(q - 1, SLOTS - 1, False)
                        if j >= 2:
                            down(q, j - 2, first)
                        elif not first:
                            down(q - 1, SLOTS - 2 + j, False)
                        if 3 <= j < 7 and not first:
                            scatter(q - 1, j - 3)
                        if j == 7:
                            pe.wait_ge(moe["d_gc"], q + 1)
                            if not first:
                                pe.wait_ge(moe["d_sc"], q * 4 - 1)
                            for g in range(2):
                                ins = pe.transpose(ps[:, 4, g * P:(g + 1) * P], G_cmb[:, g, :], ident)
                            ins.then_inc(moe["p_st"], 1)
                        if j == 8:
                            pe.wait_ge(moe["a_s"], q + 1)
                            pe.wait_ge(moe["d_g"], q + (i + 2))
                            gather(0)
                        if j == 9:
                            if not first:
                                pe.wait_ge(moe["d_sc"], q * 4)
                            gather(1)

                body(q0, True)
                with pe.Fori(0, n_more) as r:
                    body(q0 + 1 + r, False)
                last = pe.snap(q0 + n_more)
                end = done[0] = pe.snap(last + 1)
                turn(last, SLOTS - 1, False)
                down(last, SLOTS - 2, False)
                down(last, SLOTS - 1, False)
                pe.wait_ge(moe["a_xg"], end + (i + 1))
                pe.wait_ge(moe["d_xg"], end + (i + 1))
                for m in range(4):
                    scatter(last, m)

            def ffn(l):
                n0, c0 = PLAN.first[l]["ffn"], FFN0[l]
                revs = DFF // DFE

                def gate_up(it, j, first):
                    n = n0 + j
                    pe.wait_ge(slot_in[PLAN.slot[n]], it * 48 + PLAN.arrived[n])
                    if not first or j >= 3:
                        pe.wait_ge(d_act, it * SLOTS + (c0 + j - last_in(j) + 1))
                    w = ring[:, PLAN.slot[n], 0:2 * KC * P].rearrange("p (v k n) -> p v k n", v=2, k=KC)
                    for v in range(2):
                        for k in range(KC):
                            if first and j == 0 and v == 0:
                                pe.wait_ge(d_h, 8 * (2 * l + 1) + k + 1)
                                pe.wait_ge(a_h, 8 * (2 * l + 1) + k + 1)
                            ins = mm(ps[:, FB[j % 3], v * NT:(v + 1) * NT], w[:, v, k, :], hT[:, k, :],
                                     k == 0, k == KC - 1)
                    ins.then_inc(p_gu, 1)

                def down(it, j, start=False, stop=False):
                    pe.wait_ge(d_act, it * SLOTS + (c0 + j + 1))
                    w = ring[:, PLAN.slot[n0 + j], 2 * KC * P:SLOT]
                    for k in range(KC):
                        ins = mm(ps[:, 2 + k // 2, (k % 2) * NT:(k % 2 + 1) * NT], w[:, k * P:(k + 1) * P],
                                 act_s[:, j % 3, :], start and k % 2 == 0, stop, skip_group_check=True)
                    return ins.then_inc(unit_done, 1)

                gate_up(0, 0, True)
                for j in range(1, SLOTS):
                    gate_up(0, j, True)
                    down(0, j - 1, start=j == 1)
                with pe.Fori(1, revs) as it:
                    gate_up(it, 0, False)
                    down(it - 1, SLOTS - 1)
                    for j in range(1, SLOTS):
                        gate_up(it, j, False)
                        down(it, j - 1)
                down(revs - 1, SLOTS - 1, stop=True)

            for l in range(DEPTH):
                ada(l)
                norm(2 * l)
                {"dn": deltanet, "sc": shortconv, "na": attention}[KIND[l]](l)
                out_proj(l)
                norm(2 * l + 1)
                (experts if l % 2 else ffn)(l)
            pe.wait_ge(d_x, 8 * DEPTH)
            for m in range(4):
                for c in range(4):
                    g, ch = m // 2, 4 * (m % 2) + c
                    ins = pe.transpose(ps[:, [0, 1, 6, 7][m], c * P:(c + 1) * P], xT[:, ch, g * P:(g + 1) * P], ident)
                ins.then_inc(p_fin, 1)

        @block.scalar
        def _(act):
            chained = [0]

            def link(ins):
                chained[0] += 1
                ins.then_inc(a_chain, 1)
                act.wait_ge(a_chain, chained[0])

            def f(out, in_, fn, **kw):
                return act.activation(out, in_, fn, **kw)

            act.wait_ge(d_pro, 6)
            f(csil[:].rearrange("p g k -> p (g k)"), par[:, 8, 0:16], ACT.Silu).then_inc(a_pro, 1)

            def norm(s):
                for half in range(2):
                    if s > 0:
                        act.wait_ge(d_x, 4 * s - 2 + 2 * half)
                    else:
                        act.wait_ge(d_pro, 6)
                    f(hT[:, 4 * half:4 * half + 4, :], xT[:, 4 * half:4 * half + 4, :], ACT.Square).then_inc(a_sq, 1)
                act.wait_ge(p_ss, s + 1)
                link(f(rstd[:], ps[:, 7, 0:NT], ACT.Ln, scale=1.0 / DM, bias=eps[:, 0:1]))
                f(rstd[:], rstd[:], ACT.Exp, scale=-0.5).then_inc(a_rs, 1)
                l, m = s // 2, s % 2
                for k in range(KC):
                    act.wait_ge(d_h, 8 * s + k + 1)
                    f(hT[:, k, P:NT], mixT[:, k, P:NT], ACT.Identity, scale=gsc[:, m, k, 1:2],
                      bias=mod[:, 24 * m + k, 1:2]).then_inc(a_h, 1)

            def group(l, w, src, scale):
                f(SQ(l, w % 2), src, ACT.Square).then_inc(a_l2sq, 1)

            def groups(l, srcs, w0, scale, ready):
                n = len(srcs)
                for w in range(0, n + 2, 2):
                    if w < n:
                        for v in (w, w + 1):
                            ready(v)
                            if v >= 2:
                                act.wait_ge(p_l2, L20[l] + w0 + v - 1)
                            group(l, w0 + v, srcs[v], scale)
                    if w >= 2:
                        both = (w0 + w - 2, w0 + w - 1)
                        for v in both:
                            act.wait_ge(p_l2, L20[l] + v + 1)
                            if v >= 2:
                                act.wait_ge(d_l2, L20[l] + v - 1)
                            f(RS(l, v % 2), ps[:, 2 + v % 2, :], ACT.Ln, scale=scale, bias=eps[:, 0:1]) \
                                .then_inc(a_l2n, 1)
                        for v in both:
                            act.wait_ge(a_l2n, L20[l] + v + 1)
                            f(RS(l, v % 2), RS(l, v % 2), ACT.Exp, scale=-0.5).then_inc(a_l2r, 1)

            def deltanet(l):
                i = DN_LAYERS.index(l)
                u = PLAN.first[l]["in"]
                dest = [pair(t, w) for t in (qT, kT, mixT) for w in range(4)]
                act.wait_ge(d_conv, 13 * i + 1)
                for w in range(17):
                    if w < 16:
                        act.wait_ge(unit_done, u + w + 1)
                        if w < 12:
                            if w >= 2:
                                act.wait_ge(d_conv, 13 * i + w)
                            f(CB(l, w % 2).rearrange("p c g n -> p (c g) n")[:, :, 1:129], ps4(w % 2),
                              ACT.Copy).then_inc(a_pj, 1)
                        else:
                            f(pair(zT, w - 12), ps[:, w % 2, :], ACT.Silu).then_inc(a_pj, 1)
                    if 1 <= w <= 12:
                        act.wait_ge(d_conv, 13 * i + w + 1)
                        f(dest[w - 1], CY(l, (w - 1) % 2).rearrange("p c n -> p (c n)"), ACT.Silu) \
                            .then_inc(a_sl, 1)
                groups(l, [pair(qT, w) for w in range(4)] + [pair(kT, w) for w in range(4)], 0, 1.0,
                       lambda w: act.wait_ge(a_sl, SL0[l] + 12) if w == 0 else None)
                act.wait_ge(d_gate, 3 * i + 1)
                f(sv(EXPA, 16), sv(DTB, 32)[:, 0:16], ACT.Exp)
                f(sv(EB, 32), sv(BCP, 32), ACT.Exp, scale=-1.0)
                link(f(sv(AU, 32), sv(U_, 32), ACT.Abs))
                link(f(sv(EX, 32), sv(AU, 32), ACT.Exp, scale=-1.0))
                f(sv(LN1, 32), sv(EX, 32), ACT.Ln, bias=ones[:, 0:1]).then_inc(a_gate, 1)
                act.wait_ge(d_gate, 3 * i + 3)
                f(sv(EG, 32), sv(GC, 32), ACT.Exp)
                f(sv(KD, 32), sv(TG, 32), ACT.Exp).then_inc(a_gate, 1)

                def flat(t):
                    return t.rearrange("p c n -> p (c n)")

                def s_qe(h, p, hd, X, Y):
                    act.wait_ge(p_kk, hd + 1)
                    f(QE(l, p), ps4(X)[:, 1:4:2, :], ACT.Exp).then_inc(a_qe, 1)

                def s_dec(h, p, hd, X, Y):
                    act.wait_ge(d_dec, hd + 1)
                    f(flat(TT(l, p)), flat(TT(l, p)), ACT.Exp).then_inc(a_dec, 1)

                def s_t(lev):
                    def g(h, p, hd, X, Y):
                        act.wait_ge(p_t, nth(hd, lev))
                        f(flat(TT(l, p)), ps[:, X, :], ACT.Copy).then_inc(a_t, 1)
                    return g

                def s_o(h, p, hd, X, Y):
                    act.wait_ge(p_o, hd + 1)
                    if hd >= 2:
                        act.wait_ge(state_out[p], 16 * (hd // 2))
                    f(mixT[:, h, :], ps[:, Y, 0:NT], ACT.Copy)
                    f(flat(STG(l, p)), ps[:, Y, NT:2 * NT], ACT.Copy).then_inc(a_o, 1)

                steps = [s_qe, s_dec] + [s_t(x) for x in range(LEV - 1)] + [s_o]
                for h0 in range(0, H, 2):
                    for step in steps:
                        for p in range(2):
                            step(h0 + p, p, H * i + h0 + p, 2 + 2 * p, 3 + 2 * p)
                groups(l, [pair(mixT, m) for m in range(4)], 8, 1.0 / P,
                       lambda w: act.wait_ge(a_o, H * (i + 1)) if w == 0 else None)

            def shortconv(l):
                u = PLAN.first[l]["in"]
                for j in range(4):
                    if j >= 2:
                        act.wait_ge(d_mix, MIX0[l] + j - 1)
                    for part, t in ((0, sc_b), (1, sc_c)):
                        act.wait_ge(unit_done, u + 3 * j + part + 1)
                        f(t[:, j % 2].rearrange("p c n -> p (c n)"), ps[:, (3 * j + part) % 2, :],
                          ACT.Copy).then_inc(a_pj, 1)

            def attention(l):
                u = PLAN.first[l]["in"]
                dest = [pair(t, w) for t in (qT, kT, mixT) for w in range(4)]
                for w in range(12):
                    act.wait_ge(unit_done, u + w + 1)
                    f(dest[w], ps[:, w % 2, :], ACT.Copy).then_inc(a_pj, 1)
                groups(l, [pair(qT, w) for w in range(4)] + [pair(kT, w) for w in range(4)], 0, 1.0 / HD,
                       lambda w: act.wait_ge(a_pj, PJ0[l] + 12) if w == 0 else None)

                def soft(j):
                    p = j % 2
                    act.wait_ge(p_s, j + 1)
                    if j >= 2:
                        act.wait_ge(p_pt, j - 1)
                    for hh in range(2):
                        ins = f(SS(p)[:, hh, P:3 * P], ps[:, 2 * p + hh, P:3 * P], ACT.Copy)
                    ins.then_inc(a_cp, 1)

                def expo(j):
                    p = j % 2
                    act.wait_ge(d_max, j + 1)
                    for hh in range(2):
                        for m, (x, y) in enumerate(((0, 2 * P), (2 * P, 3 * P))):
                            ins = f(SS(p)[:, hh, x:y], SS(p)[:, hh, x:y], ACT.Exp,
                                    bias=sv(MX4, 32)[:, 8 * p + 2 * m + hh:8 * p + 2 * m + hh + 1],
                                    accum_out=sv(MX4, 32)[:, 8 * p + 4 + 2 * m + hh:8 * p + 5 + 2 * m + hh])
                    ins.then_inc(a_exp, 1)

                def after(j):
                    p = j % 2
                    act.wait_ge(p_pt, j + 1)
                    f(PT(p)[:, 0, :], ps[:, 4, 0:384], ACT.Copy).then_inc(a_pt, 1)
                    act.wait_ge(p_av, j + 1)
                    f(mixT[:, j, :], ps[:, 6 + p, 0:NT], ACT.Copy).then_inc(a_mix, 1)

                soft(0)
                for j in range(KC):
                    expo(j)
                    if j + 1 < KC:
                        soft(j + 1)
                    after(j)

            done = [0]

            def experts(l):
                i, q0 = l // 2, done[0]
                act.wait_ge(moe["d_lg"], i + 1)
                f(sv(CMB, 16), sv(CMB, 16), ACT.Exp).then_inc(moe["a_lg"], 1)
                for m in range(0, 4, 2):
                    act.wait_ge(moe["p_ht"], 4 * i + m + 1)
                    f(h_tok[:, m // 2, 0:512], ps[:, 4 + m, :], ACT.Copy).then_inc(moe["a_ht"], 1)

                def tokens(q, first):
                    act.wait_ge(moe["p_ga"], q * 2 + (2 * i + 1))
                    if not first:
                        act.wait_ge(moe["p_gu"], q * SLOTS)
                    f(xg[:, 0:4, :].rearrange("p k n -> p (k n)"), ps[:, 4, :], ACT.Copy).then_inc(moe["a_xg"], 1)

                def turned(q, j, first):
                    act.wait_ge(moe["p_tr"], q * SLOTS + (j + 1))
                    if not first or j >= 2:
                        act.wait_ge(moe["p_down"], q * SLOTS + (j - 1 if j >= 2 else -j))
                    f(ma_T[:, j % 2, :], ps[:, 6 + j % 2, 0:P], ACT.Copy).then_inc(moe["a_at"], 1)

                def output(q):
                    act.wait_ge(moe["p_down"], q * SLOTS + SLOTS)
                    f(y_e[:, 0:512], ps[:, 2, :], ACT.Copy).then_inc(moe["a_y"], 1)

                def body(q, first):
                    for j in range(SLOTS):
                        act.wait_ge(moe["p_gu"], q * SLOTS + (j + 1))
                        if not first or j >= 2:
                            act.wait_ge(moe["d_act"], q * SLOTS + (j - 1 if j >= 2 else -j))
                        f(mg_s[:, j % 2, :], ps[:, j % 2, 0:P], ACT.Silu).then_inc(moe["a_silu"], 1)
                        if j >= 1:
                            turned(q, j - 1, first)
                        elif not first:
                            turned(q - 1, SLOTS - 1, False)
                        if j == 1 and not first:
                            output(q - 1)
                        if j == 7:
                            act.wait_ge(moe["p_st"], q + 1)
                            f(S_cmb, ps[:, 4, 0:NT], ACT.Copy).then_inc(moe["a_s"], 1)
                    tokens(q + 1, False)

                tokens(q0, True)
                act.wait_ge(moe["d_np"], i + 1)
                n_more = act.value_load(rounds[0:1, 0:1], min_val=NE - 1, max_val=2 * NE - 1)
                body(q0, True)
                with act.Fori(0, n_more) as r:
                    body(q0 + 1 + r, False)
                last = act.snap(q0 + n_more)
                end = done[0] = act.snap(last + 1)
                turned(last, SLOTS - 1, False)
                output(last)

            def ffn(l):
                c0 = FFN0[l]

                def unit(it, j, first):
                    act.wait_ge(p_gu, it * SLOTS + (c0 + j + 1))
                    if not first or j >= 3:
                        act.wait_ge(d_act, it * SLOTS + (c0 + j - last_in(j) + 1))
                    f(gate_s[:, j % 3, :], ps[:, FB[j % 3], 0:NT], ACT.Silu).then_inc(a_silu, 1)

                for j in range(SLOTS):
                    unit(0, j, True)
                with act.Fori(1, DFF // DFE) as it:
                    for j in range(SLOTS):
                        unit(it, j, False)

            for l in range(DEPTH):
                norm(2 * l)
                {"dn": deltanet, "sc": shortconv, "na": attention}[KIND[l]](l)
                norm(2 * l + 1)
                (experts if l % 2 else ffn)(l)

        @block.vector
        def _(dve):
            chained = [0]

            def link(ins):
                chained[0] += 1
                ins.then_inc(d_chain, 1)
                dve.wait_ge(d_chain, chained[0])

            tt, ts, stt, cp = dve.tensor_tensor, dve.tensor_scalar, dve.scalar_tensor_tensor, dve.tensor_copy

            dve.memset(eps[:], EPS)
            for b in range(4):
                dve.wait_ge(p_pro, b + 1)
                cp(pair(xT, b), ps[:, 2 + b, :]).then_inc(d_pro, 1)
            dve.wait_ge(p_pro, 5)
            dve.wait_ge(consts_in, 16)
            for k, r in enumerate(ROWS):
                ins = cp(par[:, k, 0:r], ps[:, [0, 1, 6][k // 4], (k % 4) * P:(k % 4) * P + r])
            link(ins)
            link(dve.memset(ps[:, 0:2, 0:384], 0.0))
            ts(sv(GQ, 2)[:, 0:1], ones[:, 0:1], float(HD) ** -0.5, None, ALU.mult).then_inc(d_pro, 2)

            def modulation(l):
                dve.wait_ge(d_x, 8 * l)
                for i in range(17):
                    if i < 16:
                        dve.wait_ge(unit_done, PLAN.first[l]["ada"] + i + 1)
                        if i >= 2:
                            dve.wait_ge(p_at, 16 * l + i - 1)
                        cp(ada_rows[:, i % 2, :], ps[:, i % 2, 0:384]).then_inc(d_ae, 1)
                    if i >= 1:
                        t = i - 1
                        dve.wait_ge(p_at, 16 * l + t + 1)
                        part = ps[:, 6 + t % 2, 0:384].rearrange("p (c j m) -> p c m j", c=3, j=4)
                        dve.tensor_reduce(mod[:, 3 * t:3 * t + 3, :], part[:, :, 0:2, :], AX.X, ALU.add) \
                            .then_inc(d_ar, 1)
                dve.wait_ge(d_ar, 16 * (l + 1))
                if l == 0:
                    dve.wait_ge(d_pro, 6)
                link(tt(mod[:], mod[:],
                        par[:, l, 0:48, None].to_broadcast([P, 48, 2]), ALU.add))
                for m in range(2):
                    ins = stt(gsc[:, m], mod[:, 24 * m + 8:24 * m + 16, :], 1.0,
                              par[:, l, 48 + 8 * m:56 + 8 * m, None].to_broadcast([P, KC, 2]), ALU.add, ALU.mult)
                ins.then_inc(d_mod, 1)
                dve.wait_ge(d_mod, l + 1)

            def norm(s):
                m = s % 2
                dve.wait_ge(a_rs, s + 1)
                for k in range(KC):
                    link(tt(mixT[:, k, :], xT[:, k, :], rstd[:], ALU.mult))
                    ts(hT[:, k, 0:P], mixT[:, k, 0:P], gsc[:, m, k, 0:1], mod[:, 24 * m + k, 0:1],
                       ALU.mult, ALU.add).then_inc(d_h, 1)

            def residual(b, bank, col):
                for c in range(2):
                    for g in range(2):
                        k = 2 * b + c
                        ins = stt(xT[:, k, g * P:(g + 1) * P], ps[:, bank, c * NT + g * P:c * NT + (g + 1) * P],
                                  mod[:, col + k, g:g + 1], xT[:, k, g * P:(g + 1) * P], ALU.mult, ALU.add)
                ins.then_inc(d_x, 1)

            def out_proj(l):
                for i in range(4):
                    dve.wait_ge(unit_done, PLAN.first[l]["out"] + i + 1)
                    residual(i, i % 2, 16)

            def conv(ys, xs, ws):
                def v(t):
                    return t.rearrange("p (g n) -> p g n", g=2)
                for tap, first in ((1, True), (0, False), (2, False)):
                    for c in range(2):
                        x = xs[c][:, :, tap:tap + 128]
                        if first:
                            ins = ts(v(ys[c]), x, ws[c](tap), None, ALU.mult)
                        else:
                            ins = stt(v(ys[c]), x, ws[c](tap), v(ys[c]), ALU.mult, ALU.add)
                    if tap != 2:
                        link(ins)
                return ins

            def deltanet(l):
                i = DN_LAYERS.index(l)
                if isinstance(PLAN.scratch_before[l], int):
                    dve.wait_ge(unit_done, PLAN.scratch_before[l] + 1)
                for b in range(2):
                    dve.memset(CB(l, b)[:, :, :, 0:1], 0.0)
                    ins = dve.memset(CB(l, b)[:, :, :, 129:130], 0.0)
                ins.then_inc(d_conv, 1)
                for w in range(12):
                    dve.wait_ge(a_pj, PJ0[l] + w + 1)
                    if w >= 2:
                        dve.wait_ge(a_sl, SL0[l] + w - 1)
                    b = w % 2
                    conv([CY(l, b)[:, c, :] for c in range(2)], [CB(l, b)[:, c] for c in range(2)],
                          [lambda tap, n=2 * w + c: par[:, 4 + l, 24 * tap + n:24 * tap + n + 1]
                           for c in range(2)]).then_inc(d_conv, 1)

                dve.wait_ge(p_ab, 2 * i + 1)
                ab = ps[:, 6, 0:64].rearrange("p (g d k h) -> p d g k h", g=2, d=2, k=2)
                link(cp(sv(DTB, 32), ps[:, 6, 64:96]))
                dtb = sv(DTB, 32)[:, 16:32].rearrange("p (d h) -> p d h", d=2)
                link(tt(sv(U_, 2, 2, H), ab[:, :, :, 0, :], dtb[:, :, None, :].to_broadcast([P, 2, 2, H]), ALU.add))
                cp(sv(BCP, 2, 2, H), ab[:, :, :, 1, :])
                ts(sv(MAX0, 32), sv(U_, 32), 0.0, None, ALU.max).then_inc(d_gate, 1)
                dve.wait_ge(rpb_rows, 16)
                for m in range(4):
                    dve.wait_ge(p_vt, VT0[l] + m + 1)
                    cp(vtok[:, 2 * m:2 * m + 2].rearrange("p h g n -> p (h g n)"), ps[:, 4 + m % 2, :]).then_inc(d_vt, 1)
                for w in range(8):
                    t = pair(qT if w < 4 else kT, w % 4)
                    dve.wait_ge(a_l2r, L20[l] + w + 1)
                    stt(t, t, float(P) ** -0.5 if w < 4 else 1.0, RS(l, w % 2), ALU.mult, ALU.mult).then_inc(d_l2, 1)
                dve.wait_ge(a_gate, 2 * i + 1)
                link(tt(sv(B1, 32), sv(MAX0, 32), sv(LN1, 32), ALU.add))
                expa = sv(EXPA, 16).rearrange("p (d h) -> p d h", d=2)
                for g in range(2):
                    stt(sv(G_, 2, 2, H)[:, :, g, :], sv(B1, 2, 2, H)[:, :, g, :], -1.0, expa, ALU.mult, ALU.mult)
                link(ts(sv(EB, 32), sv(EB, 32), 1.0, None, ALU.add))
                dve.reciprocal(sv(BETA, 32), sv(EB, 32)).then_inc(d_gate, 1)
                for m in range(2):
                    dve.wait_ge(p_kt, KT0[l] + m + 1)
                    cp(ktok[:, 4 * m:4 * m + 4].rearrange("p h n -> p (h n)"), ps[:, 4 + m, :]).then_inc(d_kt, 1)
                dve.wait_ge(p_ab, 2 * i + 2)
                link(cp(sv(GC, 32), ps[:, 7, 0:32]))
                tt(sv(TG, 32), ps[:, 7, 32:64], sv(GC, 32), ALU.subtract).then_inc(d_gate, 1)
                dve.wait_ge(a_gate, 2 * i + 2)
                ts(sv(NEG_EG, 32), sv(EG, 32), -1.0, None, ALU.mult)
                link(tt(sv(BKD, 32), sv(BETA, 32), sv(KD, 32), ALU.mult))

                def col(k, d, g, h):
                    n = (2 * d + g) * H + h
                    return sv(k, 32)[:, n:n + 1]

                def halves(t, m, out, op):
                    for d in range(2):
                        ins = tt(out[:, 2 * d:2 * d + 2, :], t[:, 2 * d:2 * d + 2, :],
                                 m[d][:, None, :].to_broadcast([P, 2, P]), op)
                    return ins

                def s_dec(h, p, hd, X, Y, Z):
                    dve.wait_ge(p_kk, hd + 1)
                    dve.wait_ge(a_qe, hd + 1)
                    for d in range(2):
                        for g in range(2):
                            c = 2 * d + g
                            ins = ts(TT(l, p)[:, c, :], ps[:, X, c * P:(c + 1) * P], col(GC, d, g, h), 0.0,
                                     ALU.subtract, ALU.min)
                    ins.then_inc(d_dec, 1)
                    for d in range(2):
                        ins = stt(R0(l, p)[:, d, :], ps[:, Z, d * P:(d + 1) * P], col(NEG_EG, d, 1, h),
                                  vtok[:, h, 1, :], ALU.mult, ALU.add)
                    ins.then_inc(d_r0, 1)
                    tt(QE(l, p), QE(l, p), qT[:, h, None, P:NT].to_broadcast([P, 2, P]), ALU.mult)

                def s_qd(h, p, hd, X, Y, Z):
                    dve.wait_ge(a_dec, hd + 1)
                    link(halves(TT(l, p), tri, TT(l, p), ALU.mult))
                    for d in range(2):
                        tt(QD(l, p)[:, 2 * d:2 * d + 2, :], ps4(Y)[:, 2:4, :], TT(l, p)[:, 2 * d:2 * d + 2, :], ALU.mult)
                        for g in range(2):
                            c = 2 * d + g
                            ins = stt(AT(l, p)[:, c, :], ps4(Y)[:, g, :], col(BETA, d, g, h), TT(l, p)[:, c, :],
                                      ALU.mult, ALU.mult)
                    link(ins)
                    link(halves(AT(l, p), level(0, True), MM(l, p), ALU.mult))
                    tt(UU(l, p), ident[:, None, :].to_broadcast([P, 4, P]), MM(l, p), ALU.subtract).then_inc(d_qd, 1)

                def s_m(lev):
                    def f(h, p, hd, X, Y, Z):
                        dve.wait_ge(p_m, nth(hd, lev - 1))
                        halves(ps4(X), level(lev), MM(l, p), ALU.mult).then_inc(d_m, 1)
                    return f

                def s_u(lev):
                    def f(h, p, hd, X, Y, Z):
                        dve.wait_ge(p_mu, nth(hd, lev - 1))
                        tt(UU(l, p), UU(l, p), ps4(Y), ALU.subtract).then_inc(d_u, 1)
                    return f

                def s_y(h, p, hd, X, Y, Z):
                    dve.wait_ge(p_y, hd + 1)
                    cp(MM(l, p), ps4(X)).then_inc(d_y, 1)

                def s_z(h, p, hd, X, Y, Z):
                    dve.wait_ge(p_z, hd + 1)
                    cp(TT(l, p)[64:128, 0:2, :], ps4(Y)[64:128, 0:2, :])
                    cp(TT(l, p)[0:64, 2:4, :], ps4(Y)[0:64, 2:4, :]).then_inc(d_z, 1)

                def s_v(h, p, hd, X, Y, Z):
                    dve.wait_ge(p_tz, hd + 1)
                    m = MM(l, p)
                    tt(m[64:128, 0:2, :], m[64:128, 0:2, :], ps4(X)[64:128, 0:2, :], ALU.subtract)
                    link(tt(m[0:64, 2:4, :], m[0:64, 2:4, :], ps4(X)[0:64, 2:4, :], ALU.subtract))
                    for d in range(2):
                        ts(VS(l, p)[:, d, :], m[:, 2 * d, :], col(BKD, d, 0, h), None, ALU.mult)
                    for d in range(2):
                        for g in range(2):
                            c = 2 * d + g
                            ins = ts(m[:, c, :], m[:, c, :], col(BETA, d, g, h), None, ALU.mult)
                    ins.then_inc(d_v, 1)

                steps = [s_dec, s_qd]
                for lev in range(1, LEV):
                    steps += [s_m(lev), s_u(lev)]
                steps += [s_y, s_z, s_v]
                for h0 in range(0, H, 2):
                    for step in steps:
                        for p in range(2):
                            step(h0 + p, p, H * i + h0 + p, 2 + 2 * p, 3 + 2 * p, 6 + p)
                for m in range(4):
                    dve.wait_ge(a_l2r, L20[l] + 8 + m + 1)
                    t = pair(mixT, m)
                    ins = stt(t, t, par[:, 4 + l, 72:73], RS(l, m % 2), ALU.mult, ALU.mult)
                    ins.then_inc(d_l2, 1)
                    dve.wait_ge(d_l2, L20[l] + 8 + m + 1)
                    tt(t, t, pair(zT, m), ALU.mult).then_inc(d_mix, 1)

            def shortconv(l):
                u = PLAN.first[l]["in"]
                for b in range(2):
                    dve.memset(sc_cu[:, b, :, :, 0:1], 0.0)
                    ins = dve.memset(sc_cu[:, b, :, :, 129:130], 0.0)
                link(ins)
                for j in range(4):
                    b = j % 2
                    dve.wait_ge(a_pj, PJ0[l] + 2 * j + 2)
                    dve.wait_ge(unit_done, u + 3 * j + 3)
                    tt(sc_cu[:, b].rearrange("p c g n -> p (c g) n")[:, :, 1:129],
                       sc_c[:, b].rearrange("p c (g n) -> p (c g) n", g=2), ps4((3 * j + 2) % 2),
                       ALU.mult).then_inc(d_prod, 1)
                    dve.wait_ge(d_prod, j + 1)
                    link(conv([sc_y[:, b, c, :] for c in range(2)], [sc_cu[:, b, c] for c in range(2)],
                               [lambda tap, n=2 * j + c: par[:, 5, 8 * tap + n:8 * tap + n + 1]
                                for c in range(2)]))
                    tt(mixT[:, 2 * j:2 * j + 2, :], sc_y[:, b], sc_b[:, b], ALU.mult).then_inc(d_mix, 1)

            def attention(l):
                dve.wait_ge(bias_in, 64)
                link(tt(na_bias, na_bias, cst[:, None, C_NAM:C_NAM + P].to_broadcast([P, NH, P]), ALU.add))
                for m in range(2):
                    dve.wait_ge(p_ct, m + 1)
                    cp(kctxT[:, 4 * m:4 * m + 4, :].rearrange("p c n -> p (c n)"), ps[:, 6 + m, :]).then_inc(d_ct, 1)
                for m in range(4):
                    dve.wait_ge(p_vt, VT0[l] + m + 1)
                    cp(na_vtok[:, m // 2, 512 * (m % 2):512 * (m % 2) + 512], ps[:, 4 + m % 2, :]).then_inc(d_vt, 1)
                link(ts(sv(GQ, 2)[:, 1:2], par[:, 6, 0:1], sv(GQ, 2)[:, 0:1], None, ALU.mult))
                for w in range(8):
                    t = pair(qT if w < 4 else kT, w % 4)
                    dve.wait_ge(a_l2r, L20[l] + w + 1)
                    stt(t, t, sv(GQ, 2)[:, 1:2] if w < 4 else par[:, 6, 1:2], RS(l, w % 2),
                        ALU.mult, ALU.mult).then_inc(d_l2, 1)
                for m in range(2):
                    dve.wait_ge(p_kt, KT0[l] + m + 1)
                    cp(ktok_na[:, 512 * m:512 * m + 512], ps[:, 4 + m, :]).then_inc(d_kt, 1)

                def local(j):
                    p = j % 2
                    dve.wait_ge(p_s, j + 1)
                    dve.wait_ge(a_cp, j + 1)
                    for hh in range(2):
                        ins = tt(SS(p)[:, hh, 0:P], ps[:, 2 * p + hh, 0:P], na_bias[:, 2 * j + hh, :], ALU.add)
                    ins.then_inc(d_loc, 1)
                    dve.wait_ge(d_loc, j + 1)
                    mx = sv(MX4, 32)[:, 8 * p:8 * p + 4]
                    dve.tensor_reduce(mx[:, 0:2], SS(p)[:, :, 0:2 * P], AX.X, ALU.max)
                    link(dve.tensor_reduce(mx[:, 2:4], SS(p)[:, :, 2 * P:3 * P], AX.X, ALU.max))
                    ts(mx, mx, -1.0, None, ALU.mult).then_inc(d_max, 1)

                def weigh(j):
                    p = j % 2
                    dve.wait_ge(a_exp, j + 1)
                    su = sv(MX4, 32)[:, 8 * p + 4:8 * p + 8]
                    link(dve.reciprocal(su, su))
                    for hh in range(2):
                        for m, (x, y) in enumerate(((0, 2 * P), (2 * P, 3 * P))):
                            ins = ts(SS(p)[:, hh, x:y], SS(p)[:, hh, x:y], su[:, 2 * m + hh:2 * m + hh + 1], None,
                                     ALU.mult)
                    ins.then_inc(d_p, 1)

                local(0)
                for j in range(KC):
                    if j + 1 < KC:
                        local(j + 1)
                    weigh(j)
                    dve.wait_ge(p_pt, j + 1)
                    cp(PT(j % 2)[:, 1, :], ps[:, 5, 0:384]).then_inc(d_pt, 1)

            done = [0]

            def routing(l):
                i = l // 2
                dve.wait_ge(moe["p_rt"], 2 * i + 1)
                lg, e = sv(LG, 2, NE), sv(CMB, 2, NE)
                link(cp(sv(LG, 16), ps[:, 2, 0:16]))
                shape = [P, 2, NE, NE]
                other = lg[:, :, None, :].to_broadcast(shape)
                own = lg[:, :, :, None].to_broadcast(shape)
                tt(rk[:, 0], other, own, ALU.is_gt)
                link(tt(rk[:, 1], other, own, ALU.is_equal))
                lower = cst[:, C_RK:C_RK + 64].rearrange("p (e f) -> p e f", e=NE)
                for g in range(2):
                    ins = tt(rk[:, 1, g], rk[:, 1, g], lower, ALU.mult)
                link(ins)
                link(tt(rk[:, 0], rk[:, 0], rk[:, 1], ALU.add))
                sel, mx = sv(SEL, 16), sv(MX, 4)
                dve.tensor_reduce(sel, rk[:, 0].rearrange("p g e f -> p (g e) f"), AX.X, ALU.add)
                link(dve.tensor_reduce(mx[:, 0:2], lg, AX.X, ALU.max))
                ts(sel, sel, float(TOP_K), None, ALU.is_lt).then_inc(moe["d_sel"], 1)
                dve.wait_ge(moe["d_sel"], i + 1)
                tt(e, lg, mx[:, 0:2, None].to_broadcast([P, 2, NE]), ALU.subtract).then_inc(moe["d_lg"], 1)
                dve.wait_ge(moe["a_lg"], i + 1)
                link(tt(sv(CMB, 16), sv(CMB, 16), sel, ALU.mult))
                link(dve.tensor_reduce(mx[:, 2:4], e, AX.X, ALU.add))
                link(dve.reciprocal(mx[:, 2:4], mx[:, 2:4]))
                link(dve.memset(combv, 0.0))
                link(dve.memset(slotv, -1.0))
                for half in range(2):
                    c = slice(NE * half, NE * half + NE)
                    tt(combv[:, :, c], e, mx[:, 2:4, None].to_broadcast([P, 2, NE]), ALU.mult)
                dve.wait_ge(moe["p_rt"], 2 * i + 2)
                link(tt(slotv[:, :, 0:NE], ps[:, 3, 0:16].rearrange("p (g e) -> p g e", g=2),
                        sv(SEL, 2, NE), ALU.mult))
                link(ts(slotv[:, :, 0:NE], slotv[:, :, 0:NE], -1.0, None, ALU.add))
                ts(slotv[:, :, NE:2 * NE], slotv[:, :, 0:NE], -float(P), None, ALU.add)
                ts(iota, ps[:, 3, P:2 * P], -1.0, None, ALU.add)
                link(dve.tensor_reduce(mx[:, 0:1], ps[:, 3, 16:24], AX.X, ALU.max))
                link(ts(mx[:, 1:2], mx[:, 0:1], float(P), float(NE), ALU.is_gt, ALU.mult))
                ts(rounds, mx[:, 1:2], float(NE - 1), None, ALU.add).then_inc(moe["d_np"], 1)
                dve.wait_ge(moe["d_np"], i + 1)
                for m in range(1, 4, 2):
                    dve.wait_ge(moe["p_ht"], 4 * i + m + 1)
                    cp(h_tok[:, m // 2, 512:1024], ps[:, 4 + m, :]).then_inc(moe["d_ht"], 1)

            def experts(l):
                i, q0 = l // 2, done[0]
                routing(l)

                def col(t, g, q):
                    return t[:, g, q:q + 1] if isinstance(q, int) else t[:, g, bass.ds(q, 1)]

                def chosen(q, r, first):
                    if not first:
                        dve.wait_ge(moe["p_ga"], q * 2 + 2 * i)
                    for g in range(2):
                        ins = ts(G_sel[:, g, :], iota, col(slotv, g, r), None, ALU.is_equal)
                    ins.then_inc(moe["d_g"], 1)

                def weighted(q, r, first):
                    if not first:
                        dve.wait_ge(moe["p_st"], q)
                    for g in range(2):
                        ins = ts(G_cmb[:, g, :], iota, col(slotv, g, r), col(combv, g, r),
                                 ALU.is_equal, ALU.mult)
                    ins.then_inc(moe["d_gc"], 1)

                def tokens(q, first):
                    dve.wait_ge(moe["p_ga"], q * 2 + (2 * i + 2))
                    if not first:
                        dve.wait_ge(moe["p_gu"], q * SLOTS)
                    cp(xg[:, 4:8, :].rearrange("p k n -> p (k n)"), ps[:, 5, :]).then_inc(moe["d_xg"], 1)

                def output(q):
                    dve.wait_ge(moe["p_down"], q * SLOTS + SLOTS)
                    cp(y_e[:, 512:1024], ps[:, 3, :]).then_inc(moe["d_y"], 1)

                def add_up(q, m):
                    dve.wait_ge(moe["p_sc"], q * 4 + (m + 1))
                    t = pair(y_sum, m)
                    tt(t, t, ps[:, 4 + m % 2, :], ALU.add).then_inc(moe["d_sc"], 1)

                def body(r, first):
                    q = q0 + r
                    for j in range(SLOTS):
                        dve.wait_ge(moe["a_silu"], q * SLOTS + (j + 1))
                        if not first or j >= 2:
                            dve.wait_ge(moe["p_tr"], q * SLOTS + (j - 1 if j >= 2 else -j))
                        tt(ma_s[:, j % 2, :], mg_s[:, j % 2, :], ps[:, j % 2, P:2 * P], ALU.mult) \
                            .then_inc(moe["d_act"], 1)
                        if j == 1 and not first:
                            output(q - 1)
                        if 3 <= j < 7 and not first:
                            add_up(q - 1, j - 3)
                        if j == 5:
                            weighted(q, r, first)
                        if j == 6:
                            chosen(q + 1, r + 1, False)
                    tokens(q + 1, False)

                chosen(q0, 0, True)
                link(dve.memset(y_sum, 0.0))
                tokens(q0, True)
                n_more = dve.value_load(rounds[0:1, 0:1], min_val=NE - 1, max_val=2 * NE - 1)
                body(0, True)
                with dve.Fori(0, n_more) as r:
                    body(r + 1, False)
                last = dve.snap(q0 + n_more)
                end = done[0] = dve.snap(last + 1)
                output(last)
                for m in range(4):
                    add_up(last, m)
                dve.wait_ge(moe["d_sc"], end * 4)
                for b in range(4):
                    for k in (2 * b, 2 * b + 1):
                        for g in range(2):
                            t = slice(g * P, (g + 1) * P)
                            ins = stt(xT[:, k, t], y_sum[:, k, t], mod[:, 40 + k, g:g + 1], xT[:, k, t],
                                      ALU.mult, ALU.add)
                    ins.then_inc(d_x, 1)

            def ffn(l):
                c0, revs = FFN0[l], DFF // DFE

                def unit(it, j, first):
                    dve.wait_ge(a_silu, it * SLOTS + (c0 + j + 1))
                    if not first or j >= 3:
                        dve.wait_ge(unit_done, it * SLOTS + (PLAN.first[l]["ffn"] + j - last_in(j) + 1))
                    tt(act_s[:, j % 3, :], gate_s[:, j % 3, :], ps[:, FB[j % 3], NT:2 * NT], ALU.mult) \
                        .then_inc(d_act, 1)

                for j in range(SLOTS):
                    unit(0, j, True)
                with dve.Fori(1, revs) as it:
                    for j in range(SLOTS):
                        unit(it, j, False)
                dve.wait_ge(unit_done, PLAN.first[l]["ffn"] + SLOTS * revs)
                for b in range(4):
                    residual(b, 2 + b, 40)

            for l in range(DEPTH):
                modulation(l)
                norm(2 * l)
                {"dn": deltanet, "sc": shortconv, "na": attention}[KIND[l]](l)
                out_proj(l)
                norm(2 * l + 1)
                (experts if l % 2 else ffn)(l)
            for m in range(4):
                dve.wait_ge(p_fin, m + 1)
                cp(xtok[:, m // 2, 512 * (m % 2):512 * (m % 2) + 512], ps[:, [0, 1, 6, 7][m], :]).then_inc(d_fin, 1)


_INS = ["x_prompt", "x_sample", "state_dn", "cache_na_k", "cache_na_v", "c", "c_ctx", "ada_w", "ada_b",
        "norm_mix", "norm_ffn", "dn_w_in", "dn_w_ab", "dn_conv", "dn_a_log", "dn_dt_bias", "dn_norm",
        "dn_w_out", "sc_w_in", "sc_conv", "sc_w_out", "na_w_qkv", "na_q_norm", "na_k_norm", "na_rpb",
        "na_w_out", "ff_w_gu", "ff_w_down", "moe_router", "moe_w_gu", "moe_w_down"]
_OUTS = [(1, T, DM), (1, T, DM), (1, 2, 2, H, P, P), (1, 1, NH, T, HD), (1, 1, NH, T, HD)]


def kernel(**inputs):
    import concourse.bacc as bacc
    from concourse.bass_utils import run_bass_kernel_spmd as run

    nc = bacc.Bacc("TRN2", target_bir_lowering=False, num_devices=1)
    arrays, args = {}, {}
    for name in _INS + ["consts"]:
        x = shape_constants() if name == "consts" else np.ascontiguousarray(inputs[name])
        arrays[f"in_{name}"] = x
        args[name] = nc.dram_tensor(f"in_{name}", x.shape, mybir.dt.from_np(x.dtype), kind="ExternalInput").ap()
    outs = [nc.dram_tensor(f"out_{i}", shape, F32, kind="ExternalOutput").ap() for i, shape in enumerate(_OUTS)]
    trunk(nc, args, outs)
    r = run(nc, [arrays], core_ids=[0])
    return tuple(r.results[0][f"out_{i}"] for i in range(len(_OUTS)))
```
